# Optimizing a Trainium2 kernel written in Bass

```python
import jax, jax.numpy as jnp
from jax import lax
import numpy as np

D_MODEL = 1024
BATCH = 1
SEQ = 512
DEPTH = 2

CHUNK = 128
SGU_GROUPS = 8
SGU_WIDTH = D_MODEL
SGU_GROUP_DIM = SGU_WIDTH // SGU_GROUPS
SB_HEADS = 8
SB_HEAD_DIM = 128
SB_WIDTH = SB_HEADS * SB_HEAD_DIM
Q_BLOCK = 128
D_FF = 4 * D_MODEL
CONV_WIDTH = 3
N_MOD = 6
EPS = 1e-6
IN_COLS = 2 * SGU_WIDTH + 3 * SB_WIDTH + 2 * D_MODEL

kernel_name = "hybrid_sgu_stickbreaking_convffn_trunk"

def _rmsnorm(x, g):
    xf = x.astype(jnp.float32)
    y = xf * lax.rsqrt(jnp.mean(xf * xf, axis=-1, keepdims=True) + EPS)
    return (y * g.astype(jnp.float32)).astype(x.dtype)

def _layernorm(x, g):
    xf = x.astype(jnp.float32)
    mu = jnp.mean(xf, axis=-1, keepdims=True)
    var = jnp.mean(jnp.square(xf - mu), axis=-1, keepdims=True)
    return ((xf - mu) * lax.rsqrt(var + EPS) * g.astype(jnp.float32)).astype(x.dtype)

def _modulate(h, shift, scale):
    return h * (1.0 + scale[:, None, :]) + shift[:, None, :]

def _chunked_sgu(u, v, g_sgu, w_spatial, b_spatial):
    b, s, _ = v.shape
    vn = _layernorm(v, g_sgu)
    vc = vn.reshape(b, s // CHUNK, CHUNK, SGU_GROUPS, SGU_GROUP_DIM)
    causal = jnp.tril(jnp.ones((CHUNK, CHUNK), dtype=bool))
    w_masked = jnp.where(causal[None], w_spatial, 0.0).astype(v.dtype)
    f = jnp.einsum('gts,bcsgd->bctgd', w_masked, vc)
    f = f + jnp.transpose(b_spatial, (1, 0)).astype(v.dtype)[None, None, :, :, None]
    return u * f.reshape(b, s, SGU_WIDTH)

def _stick_breaking_attention(q, k, v):
    b, h, s, dh = q.shape
    nb = s // Q_BLOCK
    scale = SB_HEAD_DIM ** -0.5
    qf = q.astype(jnp.float32) * scale
    kf = k.astype(jnp.float32)
    vf = v.astype(jnp.float32)
    outs = []
    for i in range(nb):
        kv_len = (i + 1) * Q_BLOCK
        qb = qf[:, :, i * Q_BLOCK:kv_len]
        z = jnp.einsum('bhqd,bhkd->bhqk', qb, kf[:, :, :kv_len])
        q_pos = i * Q_BLOCK + jnp.arange(Q_BLOCK)
        mask = jnp.arange(kv_len)[None, :] < q_pos[:, None]
        log_1m_beta = jnp.where(mask, jax.nn.log_sigmoid(-z), 0.0)
        suffix = lax.cumsum(log_1m_beta, axis=3, reverse=True)
        attn = jnp.exp(jnp.where(mask, z + suffix, -jnp.inf))
        outs.append(jnp.einsum('bhqk,bhkd->bhqd', attn, vf[:, :, :kv_len]))
    out = jnp.concatenate(outs, axis=2)
    out = jnp.transpose(out, (0, 2, 1, 3)).reshape(b, s, h * dh)
    return out.astype(v.dtype)

def _token_mixer(h, w_in, g_sgu, w_spatial, b_spatial, w_a_out, w_b_out, w_o):
    b, s, _ = h.shape
    proj = h @ w_in
    split_at = np.cumsum([SGU_WIDTH, SGU_WIDTH, SB_WIDTH, SB_WIDTH, SB_WIDTH, D_MODEL])
    u_a, v_a, q_b, k_b, v_b, gate_a, gate_b = jnp.split(proj, split_at, axis=-1)
    y_a = _chunked_sgu(jax.nn.gelu(u_a, approximate=False), jax.nn.gelu(v_a, approximate=False),
                       g_sgu, w_spatial, b_spatial) @ w_a_out
    to_heads = lambda t: jnp.transpose(t.reshape(b, s, SB_HEADS, SB_HEAD_DIM), (0, 2, 1, 3))
    y_b = _stick_breaking_attention(to_heads(q_b), to_heads(k_b), to_heads(v_b)) @ w_b_out
    merged = jax.nn.sigmoid(gate_a) * y_a + jax.nn.sigmoid(gate_b) * y_b
    return merged @ w_o

def _conv_ffn(h, w_up, conv_w, conv_b, w_down):
    s = h.shape[1]
    up = h @ w_up
    up_p = jnp.pad(up, ((0, 0), (CONV_WIDTH - 1, 0), (0, 0)))
    conv = conv_b[None, None, :]
    for kk in range(CONV_WIDTH):
        conv = conv + conv_w[kk][None, None, :] * up_p[:, kk:kk + s, :]
    a, bval = jnp.split(conv, 2, axis=-1)
    return (jax.nn.gelu(a, approximate=True) * bval) @ w_down

def setup_inputs(seed: int = 0) -> dict:
    key = jax.random.key(seed)
    ks = jax.random.split(key, 20)
    L, D = DEPTH, D_MODEL
    nrm = lambda k, shape, sc: jax.random.normal(k, shape, jnp.float32) * sc
    return {
        "x": nrm(ks[0], (BATCH, SEQ, D), 1.0),
        "c": nrm(ks[1], (BATCH, D), 1.0),
        "w_ada": nrm(ks[2], (L, D, N_MOD * D), 0.1 * D ** -0.5),
        "b_ada": nrm(ks[3], (L, N_MOD * D), 0.05),
        "g_pre_mix": 1.0 + nrm(ks[4], (L, D), 0.05),
        "g_post_mix": 1.0 + nrm(ks[5], (L, D), 0.05),
        "g_pre_ffn": 1.0 + nrm(ks[6], (L, D), 0.05),
        "g_post_ffn": 1.0 + nrm(ks[7], (L, D), 0.05),
        "w_in": nrm(ks[8], (L, D, IN_COLS), D ** -0.5),
        "g_sgu": 1.0 + nrm(ks[9], (L, SGU_WIDTH), 0.05),
        "w_spatial": nrm(ks[10], (L, SGU_GROUPS, CHUNK, CHUNK), CHUNK ** -0.5),
        "b_spatial": 1.0 + nrm(ks[11], (L, SGU_GROUPS, CHUNK), 0.1),
        "w_a_out": nrm(ks[12], (L, SGU_WIDTH, D), SGU_WIDTH ** -0.5),
        "w_b_out": nrm(ks[13], (L, SB_WIDTH, D), SB_WIDTH ** -0.5),
        "w_o": nrm(ks[14], (L, D, D), D ** -0.5),
        "w_up": nrm(ks[15], (L, D, 2 * D_FF), D ** -0.5),
        "conv_w": nrm(ks[16], (L, CONV_WIDTH, 2 * D_FF), CONV_WIDTH ** -0.5),
        "conv_b": nrm(ks[17], (L, 2 * D_FF), 0.02),
        "w_down": nrm(ks[18], (L, D_FF, D), D_FF ** -0.5),
    }

def reference(x, c, w_ada, b_ada, g_pre_mix, g_post_mix, g_pre_ffn, g_post_ffn,
              w_in, g_sgu, w_spatial, b_spatial, w_a_out, w_b_out, w_o,
              w_up, conv_w, conv_b, w_down):
    c_act = jax.nn.silu(c)
    for l in range(DEPTH):
        mod = c_act @ w_ada[l] + b_ada[l]
        shift_m, scale_m, gate_m, shift_f, scale_f, gate_f = jnp.split(mod, N_MOD, axis=-1)
        h = _modulate(_rmsnorm(x, g_pre_mix[l]), shift_m, scale_m)
        y = _token_mixer(h, w_in[l], g_sgu[l], w_spatial[l], b_spatial[l],
                         w_a_out[l], w_b_out[l], w_o[l])
        x = x + (1.0 + gate_m)[:, None, :] * _rmsnorm(y, g_post_mix[l])
        h = _modulate(_rmsnorm(x, g_pre_ffn[l]), shift_f, scale_f)
        y = _conv_ffn(h, w_up[l], conv_w[l], conv_b[l], w_down[l])
        x = x + (1.0 + gate_f)[:, None, :] * _rmsnorm(y, g_post_ffn[l])
    return x


_drawn_inputs = setup_inputs


def setup_inputs(seed=0):
    import zlib

    import numpy as np

    out = dict(_drawn_inputs(seed))
    spreads = {}
    factors = {}
    for name, (base, spread) in spreads.items():
        noise = np.random.default_rng([zlib.crc32(name.encode()), seed]).standard_normal(out[name].shape)
        drawn = base * np.exp(spread * noise) if base else spread * noise
        out[name] = __import__('jax').numpy.asarray(drawn.astype(out[name].dtype))
    for name, factor in factors.items():
        out[name] = (out[name] * factor).astype(out[name].dtype)
    return out
```

```python
from contextlib import ExitStack

import concourse.bass as bass
from concourse import mybir

F32 = mybir.dt.float32
F32R = mybir.dt.float32r
BF16 = mybir.dt.bfloat16
ALU = mybir.AluOpType
ACT = mybir.ActivationFunctionType

P = 128
D = 1024
S = 512
DEPTH = 2
KT = D // P
NC = S // P
HEADS = 8
DFF = 4 * D
QUARTERS = 4
PAIRS = DFF // P
SCALE = float(P) ** -0.5
EPS = 1e-6

U_V = 0
U_U = U_V + KT
U_HEAD = U_U + KT
U_GA = U_HEAD + 4 * HEADS
U_GB = U_GA + KT
U_O = U_GB + 2 * KT
U_FFN = U_O + KT
UPQ = PAIRS // QUARTERS
FQ = 2 * UPQ + KT
UNITS = U_FFN + QUARTERS * FQ
RING = 4
RAW = 2
AHEAD = 2

C_BADA = 0
C_GPREM = 48
C_GPOSTM = 56
C_GPREF = 64
C_GPOSTF = 72
C_GSGU = 80
C_CB = 88
C_CW = C_CB + 2 * PAIRS
COLS = C_CW + 3 * 2 * PAIRS
SHIFT_M, SCALE_M, GATE_M, SHIFT_F, SCALE_F, GATE_F = (8 * i for i in range(6))
MODS = 48
ADA_FIRST = 16


def n_keys(j):
    return S - P * j


def build(nc, xT, cvec, w_stream, w_ada, cols_d, w_sp, b_sp, outT):
    with ExitStack() as ctx:
        def sb(name, shape, dt=F32):
            return ctx.enter_context(nc.sbuf_tensor(name, shape, dt))

        def sem(name):
            return ctx.enter_context(nc.semaphore(name))

        X = sb("X", [P, KT, S])
        HH, HL = sb("HH", [P, KT, S], F32R), sb("HL", [P, KT, S], F32R)
        AH, AL = sb("AH", [P, KT, S], F32R), sb("AL", [P, KT, S], F32R)
        OH, OL = sb("OH", [P, KT, S], F32R), sb("OL", [P, KT, S], F32R)
        M = sb("M", [P, KT, S])
        raw = sb("raw", [P, RAW, D])
        WH, WL = sb("WH", [P, RING, KT, P], F32R), sb("WL", [P, RING, KT, P], F32R)
        SC = sb("SC", [P, 14 * S], F32R)
        T = sb("T", [P, 5, S])
        ada = sb("ada", [P, D])
        cact = sb("cact", [P, D])
        cols = sb("cols", [P, DEPTH * COLS])
        mod = sb("mod", [P, DEPTH * MODS])
        acc = sb("acc", [P, 4])
        coef = sb("coef", [P, 2, KT])
        eps = sb("eps", [P, 1])
        ident = sb("ident", [P, P])
        ones = sb("ones", [P, P])
        tmp_tri = sb("tmp_tri", [P, P])
        ntri, nones = sb("ntri", [P, P], F32R), sb("nones", [P, P], F32R)
        strict, negm = sb("strict", [P, P], BF16), sb("negm", [P, P], BF16)
        stats = sb("stats", [P, NC, 2, 6])
        mv = sb("mv", [P, NC, 2])
        rstd = sb("rstd", [P, NC])

        off = {j: sum(n_keys(i) for i in range(j)) for j in range(NC)}
        SPH = {j: SC[:, off[j]:off[j] + n_keys(j)] for j in range(NC)}
        SPL = {j: SC[:, 1280 + off[j]:1280 + off[j] + n_keys(j)] for j in range(NC)}
        ATH = {j: SPH[0] if j == 0 else SC[:, 2560 + off[j] - S:2560 + off[j] - S + n_keys(j)] for j in range(NC)}
        ATL = {j: SPL[0] if j == 0 else SC[:, 3328 + off[j] - S:3328 + off[j] - S + n_keys(j)] for j in range(NC)}
        QH, QL, KH, KL, VH, VL = (SC[:, 4096 + S * i:4096 + S * (i + 1)] for i in range(6))
        WSH, WSL = SC[:, 0:D], SC[:, D:2 * D]
        M_tok = M[:, :, :].rearrange("p m t -> p (m t)").rearrange("p (c d) -> p c d", c=NC)
        VA = {True: AH, False: AL}

        ps = [ctx.enter_context(nc.psum_tensor(f"ps{i}", [P, S], F32)) for i in range(8)]

        w_landed = [sem(f"w_landed{i}") for i in range(RAW)]
        w_hi, w_split, unit_done = sem("w_hi"), sem("w_split"), sem("unit_done")
        x_landed, cols_landed, c_landed = sem("x_landed"), sem("cols_landed"), sem("c_landed")
        ada_landed, ada_used, ada_bias = sem("ada_landed"), sem("ada_used"), sem("ada_bias")
        ada0_landed = [sem(f"ada0_landed{i}") for i in range(4)]
        c_ready = sem("c_ready")
        bsp_landed, ws_landed = sem("bsp_landed"), sem("ws_landed")
        pool_consts, dve_consts = sem("pool_consts"), sem("dve_consts")
        ws_split = sem("ws_split")
        coef_ready = sem("coef_ready")
        xsq, xsum, xroot, xnorm, h_mod, h_hi, h_ready = (sem(n) for n in (
            "xsq", "xsum", "xroot", "xnorm", "h_mod", "h_hi", "h_ready"))
        y_sumsq, y_sum, y_root, x_new = (sem(n) for n in ("y_sumsq", "y_sum", "y_root", "x_new"))
        v_gelu, v_tr, v_copied = sem("v_gelu"), sem("v_tr"), sem("v_copied")
        ln_var, ln_root, vn_ready = sem("ln_var"), sem("ln_root"), sem("vn_ready")
        u_gelu, f_done, a_ready = sem("u_gelu"), sem("f_done"), sem("a_ready")
        q_evac, k_evac, vb_evac, ao_evac = sem("q_evac"), sem("k_evac"), sem("vb_evac"), sem("ao_evac")
        q_split, k_split, vb_tr, vb_split = sem("q_split"), sem("k_split"), sem("vb_tr"), sem("vb_split")
        z_done, ln1p, sp_ready, sfx = sem("z_done"), sem("ln1p"), sem("sp_ready"), sem("sfx")
        arg_masked, attn32, attn_ready = sem("arg_masked"), sem("attn32"), sem("attn_ready")
        av_done, o_split = sem("av_done"), sem("o_split")
        ga_sig, ga_used = sem("ga_sig"), sem("ga_used")
        gb_sig, merged = sem("gb_sig"), sem("merged")
        wo_evac, wo_acc = sem("wo_evac"), sem("wo_acc")
        tap2, conved, gelued, g_ready = sem("tap2"), sem("conved"), sem("gelued"), sem("g_ready")
        dn_added, dn_sq, dn_acc = sem("dn_added"), sem("dn_sq"), sem("dn_acc")
        out_landed = sem("out_landed")
        act_stage, dve_stage, pe_stage = sem("act_stage"), sem("dve_stage"), sem("pe_stage")

        block = ctx.enter_context(nc.Block())

        def col(l, c):
            return cols[:, bass.ds(l * COLS + c, 1)]

        @block.sync
        def _(sp):
            sp.dma_start(X[:, :, :], xT).then_inc(x_landed, 16)
            for n in range(RAW):
                sp.dma_start(raw[:, n], w_stream[n]).then_inc(w_landed[n], 16)
            with sp.Fori(0, (DEPTH * UNITS - RAW) // RAW) as i:
                for s in range(RAW):
                    sp.wait_ge(w_split, i * RAW + (s + 1))
                    sp.dma_start(raw[:, s], w_stream[bass.ds(i * RAW + (s + RAW), 1)].rearrange("o p n -> (o p) n")
                                 ).then_inc(w_landed[s], 16)
            sp.wait_ge(x_new, DEPTH * 2 * KT)
            sp.dma_start(outT, X[:, :, :]).then_inc(out_landed, 16)
            sp.wait_ge(out_landed, 16)

        @block.gpsimd
        def _(pool):
            nc.gpsimd.memset(ones[:, :], 1.0).then_inc(pool_consts, 1)
            pool.wait_ge(pool_consts, 1)
            nc.gpsimd.affine_select(out=ident[:, :], in_=ones[:, :], pattern=[[-1, P]], compare_op=ALU.is_equal,
                                    fill=0.0, base=0, channel_multiplier=1)
            nc.gpsimd.affine_select(out=tmp_tri[:, :], in_=ones[:, :], pattern=[[-1, P]], compare_op=ALU.is_ge,
                                    fill=0.0, base=0, channel_multiplier=1).then_inc(pool_consts, 1)
            with pool.Fori(0, DEPTH * UNITS // RING) as i:
                for s in range(RING):
                    pool.wait_ge(w_hi, i * RING + (s + 1))
                    nc.gpsimd.tensor_tensor(WL[:, s].rearrange("p k n -> p (k n)"), raw[:, s % RAW],
                                            WH[:, s].rearrange("p k n -> p (k n)").bitcast(F32),
                                            ALU.subtract).then_inc(w_split, 1)

        @block.scalar
        def _(act):
            def split(l, n, s):
                act.wait_ge(w_landed[s % RAW], (l * (UNITS // 2) + n // 2 + 1) * 16 if isinstance(n, int)
                            else (l * (UNITS // 2) + n[0] * 2 + (n[1] // 2 + 1)) * 16)
                act.wait_ge(unit_done, l * UNITS + n + 1 if isinstance(n, int)
                            else l * UNITS + n[0] * 4 + (n[1] + 1))
                nc.scalar.activation(WH[:, s].rearrange("p k n -> p (k n)"), raw[:, s % RAW],
                                     ACT.Copy).then_inc(w_hi, 1)

            def ahead(l, i, base, s):
                split(l, (i, base + s + AHEAD), (s + AHEAD) % RING)

            def ready(l, i, base, s):
                act.wait_ge(unit_done, l * UNITS + i * 4 + (base + s + 1 + RING))

            def load_ada(l, j):
                act.wait_ge(ada_used, l * 33 + j + 2)
                act.dma_start(ada[:, :], w_ada[bass.ds(l * MODS + (j + ADA_FIRST), 1)].rearrange("o p n -> (o p) n")
                              ).then_inc(ada_landed, 16)

            def norm(l, which):
                for m in range(KT):
                    if which:
                        act.wait_ge(x_new, l * 2 * KT + m + 1)
                    nc.scalar.activation(M[:, m], X[:, m], ACT.Square).then_inc(xsq, 1)
                n = 2 * l + which
                act.wait_ge(xsum, n + 1)
                nc.scalar.activation(T[:, 3], ps[7][:, :], ACT.Sqrt, bias=eps[:, 0:1], scale=1.0 / D
                                     ).then_inc(xroot, 1)
                act.wait_ge(coef_ready, n + 1)
                shift = SHIFT_F if which else SHIFT_M
                for m in range(KT):
                    act.wait_ge(xnorm, n * KT + m + 1)
                    nc.scalar.activation(M[:, m], M[:, m], ACT.Identity, scale=coef[:, 0, m:m + 1],
                                         bias=mod[:, bass.ds(l * MODS + shift + m, 1)]).then_inc(h_mod, 1)
                    act.wait_ge(h_mod, n * KT + m + 1)
                    nc.scalar.activation(HH[:, m], M[:, m], ACT.Copy).then_inc(h_hi, 1)

            def post_root(n):
                act.wait_ge(y_sum, n + 1)
                nc.scalar.activation(T[:, 3], ps[6][:, :], ACT.Sqrt, bias=eps[:, 0:1], scale=1.0 / D
                                     ).then_inc(y_root, 1)

            act.dma_start(cact[:, :], cvec.to_broadcast([P, D])).then_inc(c_landed, 16)
            act.dma_start(cols[:, :], cols_d).then_inc(cols_landed, 16)
            M_ada = M[:, :, :].rearrange("p m t -> p (m t)").rearrange("p (s n) -> p s n", s=4)
            act.wait_ge(c_landed, 16)
            nc.scalar.activation(cact[:, :], cact[:, :], ACT.Silu).then_inc(c_ready, 1)
            for k in range(ADA_FIRST * DEPTH):
                if k >= 4:
                    act.wait_ge(ada_bias, k - 3)
                act.dma_start(M_ada[:, k % 4], w_ada[MODS * (k // ADA_FIRST) + k % ADA_FIRST]
                              ).then_inc(ada0_landed[k % 4], 16)
            act.wait_ge(ada_bias, ADA_FIRST * DEPTH)
            act.wait_ge(x_landed, 16)
            act.wait_ge(dve_consts, 1)
            act.sem_inc(act_stage, 1)
            with act.Fori(0, DEPTH) as l:
                act.wait_ge(ada_used, l * 33 + 1)
                act.dma_start(ada[:, :], b_sp[bass.ds(l, 1)].to_broadcast([P, D])).then_inc(bsp_landed, 16)
                act.dma_start(T[:, 0:2], w_sp[bass.ds(l, 1)].rearrange("o p n -> (o p) n").rearrange(
                    "p (a b) -> p a b", a=2)).then_inc(ws_landed, 16)
                for n in range(AHEAD):
                    split(l, n, n)
                norm(l, 0)

                with act.Fori(0, KT // 4) as i:
                    for s in range(4):
                        ahead(l, i, U_V, s)
                        ready(l, i, U_V, s)
                        act.wait_ge(v_tr, l * KT + i * 4 + (s + 1))
                        if s == 0:
                            act.wait_ge(ws_split, l + 1)
                        nc.scalar.activation(T[:, s], ps[s % 2][:, :], ACT.Gelu).then_inc(v_gelu, 1)
                act.wait_ge(ln_var, l + 1)
                nc.scalar.activation(rstd[:, :], mv[:, :, 1], ACT.Sqrt, bias=eps[:, 0:1]).then_inc(ln_root, 1)
                with act.Fori(0, KT // 4) as i:
                    for s in range(4):
                        ahead(l, i, U_U, s)
                        ready(l, i, U_U, s)
                        act.wait_ge(v_tr, l * KT + (s + 1 + KT))
                        act.wait_ge(a_ready, l * KT + i * 4 + (s + 1))
                        nc.scalar.activation(T[:, s], ps[s][:, :], ACT.Gelu).then_inc(u_gelu, 1)

                nc.scalar.preload_act_table_set("natural_log_exp_and_others")

                def exps(h, js):
                    for j in js:
                        act.wait_ge(arg_masked, l * 32 + h * 4 + (NC - j))
                        if j < 2:
                            act.wait_ge(attn_ready, l * 32 + h * 4 + (NC - j - 2))
                        nc.scalar.activation(T[:, 3 + j % 2, 0:n_keys(j)], ps[4 + j][:, 0:n_keys(j)],
                                             ACT.Exp).then_inc(attn32, 1)

                def head(h, first):
                    base = U_HEAD
                    ahead(l, h, base, 0)
                    ready(l, h, base, 0)
                    act.wait_ge(q_split, l * HEADS + h + 1)
                    nc.scalar.activation(T[:, 0], ps[0][:, :], ACT.Copy, scale=SCALE).then_inc(q_evac, 1)
                    load_ada(l, h * 2)
                    if not first:
                        exps(h - 1, (3, 2))
                    ahead(l, h, base, 1)
                    ready(l, h, base, 1)
                    act.wait_ge(k_split, l * HEADS + h + 1)
                    nc.scalar.activation(T[:, 1], ps[1][:, :], ACT.Copy).then_inc(k_evac, 1)
                    if not first:
                        exps(h - 1, (1, 0))
                    ahead(l, h, base, 2)
                    ready(l, h, base, 2)
                    act.wait_ge(vb_tr, l * HEADS + h + 1)
                    nc.scalar.activation(T[:, 2], ps[0][:, :], ACT.Copy).then_inc(vb_evac, 1)
                    ahead(l, h, base, 3)
                    load_ada(l, h * 2 + 1)
                    for j in (3, 2, 1, 0):
                        n = n_keys(j)
                        e = T[:, 3 + j % 2, 0:n]
                        act.wait_ge(z_done, l * 32 + h * 4 + (NC - j))
                        if j < 2:
                            act.wait_ge(sp_ready, l * 32 + h * 4 + (NC - j - 2))
                        elif not first:
                            act.wait_ge(attn_ready, l * 32 + h * 4)
                        nc.scalar.activation(e, ps[4 + j][:, 0:n], ACT.Abs)
                        act.drain()
                        nc.scalar.activation(e, e, ACT.Exp, scale=-1.0)
                        act.drain()
                        nc.scalar.activation(e, e, ACT.Ln, bias=1.0).then_inc(ln1p, 1)
                    ready(l, h, base, 3)
                    nc.scalar.activation(M[:, bass.ds(h, 1)].rearrange("p o t -> p (o t)"), ps[1][:, :],
                                         ACT.Copy).then_inc(ao_evac, 1)

                act.wait_ge(a_ready, l * KT + (KT + 4))
                head(0, True)
                with act.Fori(1, HEADS) as h:
                    head(h, False)
                exps(HEADS - 1, (3, 2, 1, 0))

                with act.Fori(0, KT // 4) as i:
                    for s in range(4):
                        ahead(l, i, U_GA, s)
                        ready(l, i, U_GA, s)
                        act.wait_ge(ga_used, l * KT + i * 4 + (s + 1))
                        if s == 3:
                            act.wait_ge(attn_ready, l * 32 + 32)
                        nc.scalar.activation(T[:, s], ps[4 + s % 2][:, :], ACT.Sigmoid).then_inc(ga_sig, 1)
                act.wait_ge(ga_used, l * KT + (KT + 4))
                act.sem_inc(act_stage, 1)
                with act.Fori(0, KT // 2) as i:
                    for s in range(4):
                        ahead(l, i, U_GB, s)
                        if s % 2 == 0:
                            ready(l, i, U_GB, s)
                            act.wait_ge(merged, l * KT + i * 2 + (s // 2 + 1))
                            nc.scalar.activation(T[:, s], ps[s][:, :], ACT.Sigmoid).then_inc(gb_sig, 1)
                        load_ada(l, i * 4 + (2 * HEADS + s))
                act.wait_ge(merged, l * KT + (KT + 2))
                act.sem_inc(act_stage, 1)
                with act.Fori(0, KT // 4) as i:
                    for s in range(4):
                        ahead(l, i, U_O, s)
                        ready(l, i, U_O, s)
                        nc.scalar.activation(M[:, bass.ds(i * 4 + s, 1)].rearrange("p o t -> p (o t)"),
                                             ps[4 + s % 2][:, :], ACT.Copy)
                        act.wait_ge(wo_acc, l * KT + i * 4 + (s + 1))
                        nc.scalar.activation(T[:, s % 2], ps[4 + s % 2][:, :], ACT.Square).then_inc(wo_evac, 1)
                post_root(2 * l)
                norm(l, 1)

                def tap(l, q, i, s):
                    tile = q * UPQ + i * 2 + (s // 2 + PAIRS * (s % 2))
                    act.wait_ge(g_ready, (l * QUARTERS + q) * UPQ + i * 2 + (s // 2 + 1))
                    nc.scalar.activation(T[:, s], ps[s][:, :], ACT.Identity, scale=col(l, tile + (C_CW + 4 * PAIRS)),
                                         bias=col(l, tile + C_CB)).then_inc(tap2, 1)

                def quarter(q, last):
                    with act.Fori(0, UPQ // 2) as i:
                        for s in range(4):
                            n = q * (FQ // 4) + i
                            ahead(l, n, U_FFN, s)
                            ready(l, n, U_FFN, s)
                            tap(l, q, i, s)
                            if s % 2:
                                act.wait_ge(conved, ((l * QUARTERS + q) * UPQ + i * 2) * 2 + (s + 4))
                                nc.scalar.activation(T[:, s - 1], T[:, s - 1], ACT.Gelu_apprx_tanh
                                                     ).then_inc(gelued, 1)
                    for i in range(KT // 4):
                        for s in range(4):
                            n = q * (FQ // 4) + (2 * UPQ // 4 + i)
                            if not last or 4 * i + s + AHEAD < KT:
                                ahead(l, n, U_FFN, s)
                            if last:
                                m = 4 * i + s
                                act.wait_ge(dn_added, l * KT * QUARTERS + (QUARTERS - 1) * KT + m + 1 + 2)
                                act.wait_ge(dn_acc, l * KT + m + 1)
                                nc.scalar.activation(T[:, s % 2], M[:, m], ACT.Square).then_inc(dn_sq, 1)

                act.wait_ge(g_ready, l * PAIRS + 2)
                act.sem_inc(act_stage, 1)
                with act.Fori(0, QUARTERS - 1) as q:
                    quarter(q, False)
                act.wait_ge(g_ready, (l + 1) * PAIRS + 2 - UPQ)
                quarter(QUARTERS - 1, True)
                post_root(2 * l + 1)
                act.wait_ge(x_new, (l + 1) * 2 * KT)

        @block.vector
        def _(dve):
            def ready(l, i, base, s):
                dve.wait_ge(unit_done, l * UNITS + i * 4 + (base + s + 1 + RING))

            def hi_lo(hi, lo, src, done):
                nc.vector.tensor_copy(hi, src)
                dve.drain()
                return nc.vector.tensor_tensor(lo, src, hi.bitcast(F32), ALU.subtract).then_inc(done, 1)

            def ada_unit(l, j):
                dve.wait_ge(ada_landed, l * 32 * 16 + (j + 1) * 16)
                nc.vector.tensor_tensor_reduce(out=ada[:, :], in0=ada[:, :], in1=cact[:, :], scale=1.0, scalar=0.0,
                                               op0=ALU.mult, op1=ALU.add, accum_out=acc[:, 0:1]).then_inc(ada_used, 1)
                dve.drain()
                nc.vector.tensor_tensor(mod[:, bass.ds(l * MODS + j + ADA_FIRST, 1)], acc[:, 0:1],
                                        col(l, j + (C_BADA + ADA_FIRST)), ALU.add)
                dve.drain()

            def modulation(l, which):
                sc, g = (SCALE_F, C_GPREF) if which else (SCALE_M, C_GPREM)
                nc.vector.scalar_tensor_tensor(out=coef[:, 0], in0=mod[:, bass.ds(l * MODS + sc, KT)], scalar=1.0,
                                               in1=cols[:, bass.ds(l * COLS + g, KT)], op0=ALU.add,
                                               op1=ALU.mult).then_inc(coef_ready, 1)

            def norm(l, which):
                n = 2 * l + which
                dve.wait_ge(xroot, n + 1)
                nc.vector.reciprocal(T[:, 3], T[:, 3])
                dve.drain()
                for m in range(KT):
                    nc.vector.tensor_tensor(M[:, m], X[:, m], T[:, 3], ALU.mult).then_inc(xnorm, 1)
                    if m:
                        dve.wait_ge(h_hi, n * KT + m)
                        nc.vector.tensor_tensor(HL[:, m - 1], M[:, m - 1], HH[:, m - 1].bitcast(F32),
                                                ALU.subtract).then_inc(h_ready, 1)
                dve.wait_ge(h_hi, n * KT + KT)
                nc.vector.tensor_tensor(HL[:, KT - 1], M[:, KT - 1], HH[:, KT - 1].bitcast(F32),
                                        ALU.subtract).then_inc(h_ready, 1)
                dve.drain()

            def post(l, which):
                gate, g = (GATE_F, C_GPOSTF) if which else (GATE_M, C_GPOSTM)
                nc.vector.scalar_tensor_tensor(out=coef[:, 1], in0=mod[:, bass.ds(l * MODS + gate, KT)], scalar=1.0,
                                               in1=cols[:, bass.ds(l * COLS + g, KT)], op0=ALU.add, op1=ALU.mult)
                dve.wait_ge(y_root, 2 * l + which + 1)
                nc.vector.reciprocal(T[:, 3], T[:, 3])
                dve.drain()
                for m in range(KT):
                    nc.vector.scalar_tensor_tensor(out=M[:, m], in0=M[:, m], scalar=coef[:, 1, m:m + 1],
                                                   in1=T[:, 3], op0=ALU.mult, op1=ALU.mult)
                    dve.drain()
                    nc.vector.tensor_tensor(X[:, m], X[:, m], M[:, m], ALU.add).then_inc(x_new, 1)
                dve.drain()

            dve.wait_ge(pool_consts, 2)
            nc.vector.memset(eps[:, :], EPS)
            nc.vector.tensor_scalar(ntri[:, :], tmp_tri[:, :], -1.0, None, ALU.mult)
            nc.vector.tensor_scalar(nones[:, :], ones[:, :], -1.0, None, ALU.mult)
            nc.vector.tensor_scalar(strict[:, :], tmp_tri[:, :], -1.0, 1.0, ALU.mult, ALU.add)
            nc.vector.tensor_scalar(negm[:, :], tmp_tri[:, :], -1e30, None, ALU.mult).then_inc(dve_consts, 1)
            dve.drain()
            M_ada = M[:, :, :].rearrange("p m t -> p (m t)").rearrange("p (s n) -> p s n", s=4)
            dve.wait_ge(cols_landed, 16)
            dve.wait_ge(c_ready, 1)
            for k in range(ADA_FIRST * DEPTH):
                dve.wait_ge(ada0_landed[k % 4], 16 * (k // 4 + 1))
                nc.vector.tensor_tensor_reduce(out=M_ada[:, k % 4], in0=M_ada[:, k % 4], in1=cact[:, :], scale=1.0,
                                               scalar=0.0, op0=ALU.mult, op1=ALU.add, accum_out=acc[:, 0:1])
                dve.drain()
                lk, jk = k // ADA_FIRST, k % ADA_FIRST
                nc.vector.tensor_tensor(mod[:, lk * MODS + jk:lk * MODS + jk + 1], acc[:, 0:1],
                                        cols[:, lk * COLS + C_BADA + jk:lk * COLS + C_BADA + jk + 1],
                                        ALU.add).then_inc(ada_bias, 1)
                dve.drain()
            dve.sem_inc(ada_used, 1)
            dve.sem_inc(v_copied, 2)
            dve.sem_inc(a_ready, 4)
            dve.sem_inc(q_split, 1)
            dve.sem_inc(k_split, 1)
            dve.sem_inc(o_split, 1)
            dve.sem_inc(vb_split, 1)
            dve.sem_inc(ga_used, 4)
            dve.sem_inc(merged, 2)
            dve.sem_inc(wo_acc, 2)
            dve.sem_inc(conved, 4)
            dve.sem_inc(g_ready, 2)
            dve.sem_inc(dn_added, 2)
            dve.sem_inc(dn_acc, 2)

            with dve.Fori(0, DEPTH) as l:
                modulation(l, 0)
                dve.wait_ge(ws_landed, l * 16 + 16)
                nc.vector.tensor_tensor(T[:, 2, 0:P], strict[:, :], ident[:, :], ALU.add)
                dve.drain()
                ws = T[:, 0:2].rearrange("p a b -> p (a b)").rearrange("p (g t) -> p g t", g=KT)
                nc.vector.tensor_tensor(ws, ws, T[:, 2, 0:P].unsqueeze(1).to_broadcast([P, KT, P]), ALU.mult)
                dve.drain()
                hi_lo(WSH, WSL, T[:, 0:2].rearrange("p a b -> p (a b)"), ws_split)
                norm(l, 0)

                with dve.Fori(0, KT // 4) as i:
                    for s in range(4):
                        dve.wait_ge(v_tr, l * KT + i * 4 + (s + 1 + 4))
                        nc.vector.tensor_copy(M_tok[:, :, bass.ds((i * 4 + s) * P, P)],
                                              ps[2 + s % 2][:, :].rearrange("p (c d) -> p c d", c=NC)
                                              ).then_inc(v_copied, 1)
                dve.drain()
                for c in range(NC):
                    for half in range(2):
                        nc.vector.bn_stats(stats[:, c, half], M_tok[:, c, half * S:(half + 1) * S])
                dve.drain()
                for c in range(NC):
                    ins = nc.vector.bn_aggr(mv[:, c], stats[:, c])
                ins.then_inc(ln_var, 1)
                dve.wait_ge(ln_root, l + 1)
                nc.vector.reciprocal(rstd[:, :], rstd[:, :])
                dve.drain()
                for c in range(NC):
                    nc.vector.tensor_scalar(M_tok[:, c], M_tok[:, c], mv[:, c, 0:1], rstd[:, c:c + 1], ALU.subtract,
                                            ALU.mult)
                dve.drain()
                for c in range(NC):
                    src = M_tok[:, c].rearrange("p (g d) -> p g d", g=KT)
                    nc.vector.tensor_copy(AH[:, :, c * P:(c + 1) * P], src)
                dve.drain()
                for c in range(NC):
                    src = M_tok[:, c].rearrange("p (g d) -> p g d", g=KT)
                    nc.vector.tensor_tensor(AL[:, :, c * P:(c + 1) * P], src,
                                            AH[:, :, c * P:(c + 1) * P].bitcast(F32),
                                            ALU.subtract).then_inc(vn_ready, 1)

                dve.wait_ge(bsp_landed, l * 16 + 16)
                dve.sem_inc(dve_stage, 1)
                with dve.Fori(0, KT // 4) as i:
                    for s in range(4):
                        g = i * 4 + s
                        dve.wait_ge(f_done, l * KT + g + 1)
                        dve.wait_ge(u_gelu, l * KT + g + 1)
                        f = ps[4 + s % 2][:, :]
                        bias = ada[:, bass.ds(g * P, P)].unsqueeze(1).to_broadcast([P, NC, P])
                        fc = f.rearrange("p (c t) -> p c t", c=NC)
                        nc.vector.scalar_tensor_tensor(out=fc, in0=fc, scalar=col(l, g + C_GSGU), in1=bias,
                                                       op0=ALU.mult, op1=ALU.add)
                        dve.drain()
                        nc.vector.tensor_tensor(T[:, s], T[:, s], f, ALU.mult)
                        dve.drain()
                        hi_lo(AH[:, bass.ds(g, 1)].rearrange("p o t -> p (o t)"),
                              AL[:, bass.ds(g, 1)].rearrange("p o t -> p (o t)"), T[:, s], a_ready)
                dve.drain().then_inc(ada_used, 1)

                def attn(h, js):
                    for j in js:
                        n = n_keys(j)
                        dve.wait_ge(sfx, l * 32 + h * 4 + (NC - j))
                        nc.vector.tensor_tensor(ps[4 + j][:, 0:P], ps[4 + j][:, 0:P], negm[:, :],
                                                ALU.add).then_inc(arg_masked, 1)
                        dve.wait_ge(attn32, l * 32 + h * 4 + (NC - j))
                        hi_lo(ATH[j], ATL[j], T[:, 3 + j % 2, 0:n], attn_ready)

                def out_split(h):
                    dve.wait_ge(av_done, l * HEADS + h + 1)
                    hi_lo(OH[:, bass.ds(h, 1)].rearrange("p o t -> p (o t)"),
                          OL[:, bass.ds(h, 1)].rearrange("p o t -> p (o t)"), ps[3][:, :], o_split)

                def head(h, first):
                    dve.wait_ge(q_evac, l * HEADS + h + 1)
                    hi_lo(QH, QL, T[:, 0], q_split)
                    if not first:
                        attn(h - 1, (3, 2))
                    dve.wait_ge(k_evac, l * HEADS + h + 1)
                    hi_lo(KH, KL, T[:, 1], k_split)
                    if not first:
                        attn(h - 1, (1, 0))
                    ada_unit(l, h * 2)
                    if not first:
                        out_split(h - 1)
                    for j in (3, 2, 1, 0):
                        n = n_keys(j)
                        e = T[:, 3 + j % 2, 0:n]
                        dve.wait_ge(ln1p, l * 32 + h * 4 + (NC - j))
                        nc.vector.scalar_tensor_tensor(out=e, in0=ps[4 + j][:, 0:n], scalar=0.0, in1=e, op0=ALU.max,
                                                       op1=ALU.add)
                        dve.drain()
                        nc.vector.tensor_tensor(e[:, 0:P], e[:, 0:P], strict[:, :], ALU.mult)
                        dve.drain()
                        hi_lo(SPH[j], SPL[j], e, sp_ready)
                    dve.wait_ge(vb_tr, l * HEADS + h + 1 + 1)
                    hi_lo(VH, VL, ps[2][:, :], vb_split)
                    ada_unit(l, h * 2 + 1)

                head(0, True)
                with dve.Fori(1, HEADS) as h:
                    head(h, False)
                attn(HEADS - 1, (3, 2, 1, 0))
                out_split(HEADS - 1)

                dve.wait_ge(ao_evac, l * HEADS + HEADS)
                dve.sem_inc(dve_stage, 1)
                with dve.Fori(0, KT // 4) as i:
                    for s in range(4):
                        m = M[:, bass.ds(i * 4 + s, 1)].rearrange("p o t -> p (o t)")
                        dve.wait_ge(ga_sig, l * KT + i * 4 + (s + 1))
                        nc.vector.tensor_tensor(m, m, T[:, s], ALU.mult).then_inc(ga_used, 1)
                dve.drain()
                with dve.Fori(0, KT // 2) as i:
                    for s in (1, 3):
                        g = i * 2 + s // 2
                        dve.wait_ge(gb_sig, l * KT + g + 1)
                        ready(l, i, U_GB, s)
                        nc.vector.tensor_tensor(T[:, s - 1], T[:, s - 1], ps[s][:, :], ALU.mult)
                        dve.drain()
                        nc.vector.tensor_tensor(T[:, s - 1], T[:, s - 1],
                                                M[:, bass.ds(g, 1)].rearrange("p o t -> p (o t)"), ALU.add)
                        dve.drain()
                        hi_lo(AH[:, bass.ds(g, 1)].rearrange("p o t -> p (o t)"),
                              AL[:, bass.ds(g, 1)].rearrange("p o t -> p (o t)"), T[:, s - 1], merged)
                        ada_unit(l, i * 4 + (2 * HEADS + s - 1))
                        ada_unit(l, i * 4 + (2 * HEADS + s))
                nc.vector.memset(T[:, 2], 0.0)
                dve.drain()
                with dve.Fori(0, KT // 4) as i:
                    for s in range(4):
                        dve.wait_ge(wo_evac, l * KT + i * 4 + (s + 1))
                        nc.vector.tensor_tensor(T[:, 2], T[:, 2], T[:, s % 2], ALU.add).then_inc(wo_acc, 1)
                        dve.drain()
                dve.drain().then_inc(y_sumsq, 1)
                post(l, 0)
                modulation(l, 1)
                norm(l, 1)

                nc.vector.memset(M[:, :, :], 0.0)

                def quarter(q, last):
                    with dve.Fori(0, UPQ // 2) as i:
                        for s in range(4):
                            tile = q * UPQ + i * 2 + (s // 2 + PAIRS * (s % 2))
                            dve.wait_ge(tap2, ((l * QUARTERS + q) * UPQ + i * 2) * 2 + (s + 1))
                            nc.vector.scalar_tensor_tensor(out=T[:, s, 1:S], in0=ps[s][:, 0:S - 1],
                                                           scalar=col(l, tile + (C_CW + 2 * PAIRS)), in1=T[:, s, 1:S],
                                                           op0=ALU.mult, op1=ALU.add)
                            dve.drain()
                            nc.vector.scalar_tensor_tensor(out=T[:, s, 2:S], in0=ps[s][:, 0:S - 2],
                                                           scalar=col(l, tile + C_CW), in1=T[:, s, 2:S],
                                                           op0=ALU.mult, op1=ALU.add).then_inc(conved, 1)
                            if s % 2:
                                g = i * 2 + s // 2
                                dve.drain()
                                dve.wait_ge(gelued, (l * QUARTERS + q) * UPQ + g + 1)
                                nc.vector.tensor_tensor(T[:, s], T[:, s - 1], T[:, s], ALU.mult)
                                dve.drain()
                                hi_lo(OH[:, bass.ds(g, 1)].rearrange("p o t -> p (o t)"),
                                      OL[:, bass.ds(g, 1)].rearrange("p o t -> p (o t)"), T[:, s], g_ready)
                    if last:
                        nc.vector.memset(T[:, 2], 0.0)
                    dve.drain()
                    for m in range(KT):
                        n = q * (FQ // 4) + (2 * UPQ // 4 + m // 4)
                        ready(l, n, U_FFN, m % 4)
                        nc.vector.tensor_tensor(M[:, m], M[:, m], ps[4 + m % 2][:, :], ALU.add).then_inc(dn_added, 1)
                        if last:
                            dve.wait_ge(dn_sq, l * KT + m + 1)
                            nc.vector.tensor_tensor(T[:, 2], T[:, 2], T[:, m % 2], ALU.add).then_inc(dn_acc, 1)
                            dve.drain()
                    dve.drain()

                with dve.Fori(0, QUARTERS - 1) as q:
                    quarter(q, False)
                quarter(QUARTERS - 1, True)
                dve.drain().then_inc(y_sumsq, 1)
                post(l, 1)

        @block.tensor
        def _(pe):
            def mm3(out, wh, wl, xh, xl, start, stop):
                nc.tensor.matmul(out, wh, xh, start=start, stop=False)
                nc.tensor.matmul(out, wh, xl, start=False, stop=False)
                return nc.tensor.matmul(out, wl, xh, start=False, stop=stop)

            def unit(l, i, base, s, bank, src):
                pe.wait_ge(w_split, l * UNITS + i * 4 + (base + s + 1))
                for k in range(KT):
                    last = mm3(ps[bank][:, :], WH[:, s, k], WL[:, s, k], src[0][:, k], src[1][:, k],
                               k == 0, k == KT - 1)
                last.then_inc(unit_done, 1)

            H, A, O = (HH, HL), (AH, AL), (OH, OL)

            def norm_sum(l, which):
                n = 2 * l + which
                for m in range(KT):
                    pe.wait_ge(xsq, n * KT + m + 1)
                    last = nc.tensor.matmul(ps[7][:, :], ones[:, :], M[:, m], start=m == 0, stop=m == KT - 1)
                last.then_inc(xsum, 1)
                pe.wait_ge(h_ready, n * KT + KT)
                pe.sem_inc(pe_stage, 1)

            def post_sum(n):
                pe.wait_ge(y_sumsq, n + 1)
                nc.tensor.matmul(ps[6][:, :], ones[:, :], T[:, 2], start=True, stop=True).then_inc(y_sum, 1)

            pe.sem_inc(unit_done, RING)
            pe.sem_inc(v_tr, 4)
            pe.sem_inc(vb_tr, 1)
            pe.wait_ge(dve_consts, 1)
            pe.sem_inc(pe_stage, 1)
            with pe.Fori(0, DEPTH) as l:
                norm_sum(l, 0)

                def v_transpose(i, s):
                    pe.wait_ge(v_gelu, l * KT + i * 4 + (s + 1))
                    pe.wait_ge(v_copied, l * KT + i * 4 + (s + 1))
                    for c in range(NC):
                        last = nc.tensor.transpose(ps[2 + s % 2][:, c * P:(c + 1) * P], T[:, s, c * P:(c + 1) * P],
                                                   ident[:, :])
                    last.then_inc(v_tr, 1)

                with pe.Fori(0, KT // 4) as i:
                    unit(l, i, U_V, 0, 0, H)
                    unit(l, i, U_V, 1, 1, H)
                    v_transpose(i, 0)
                    unit(l, i, U_V, 2, 0, H)
                    v_transpose(i, 1)
                    unit(l, i, U_V, 3, 1, H)
                    v_transpose(i, 2)
                    v_transpose(i, 3)
                pe.wait_ge(v_copied, l * KT + KT + 2)
                for i in range(KT // 4):
                    for s in range(4):
                        if i:
                            pe.wait_ge(u_gelu, l * KT + s + 1)
                        unit(l, i, U_U, s, s, H)
                    if i == 0:
                        pe.wait_ge(vn_ready, l * NC + NC)
                    for s in range(4):
                        g = 4 * i + s
                        if g >= 2:
                            pe.wait_ge(a_ready, l * KT + g - 1 + 4)
                        for c in range(NC):
                            last = mm3(ps[4 + s % 2][:, c * P:(c + 1) * P], AH[:, g, c * P:(c + 1) * P],
                                       AL[:, g, c * P:(c + 1) * P], WSH[:, g * P:(g + 1) * P],
                                       WSL[:, g * P:(g + 1) * P], True, True)
                        last.then_inc(f_done, 1)

                def suffix(h, js):
                    for j in js:
                        pe.wait_ge(sp_ready, l * 32 + h * 4 + (NC - j))
                        for k in range(j, NC):
                            at = (k - j) * P
                            for part in (SPH[k], SPL[k]):
                                last = nc.tensor.matmul(ps[4 + j][:, at:n_keys(j)],
                                                        ntri[:, :] if k == j else nones[:, :], part, start=False,
                                                        stop=True, skip_group_check=True)
                        last.then_inc(sfx, 1)

                def values(h):
                    pe.wait_ge(o_split, l * HEADS + h + 1)
                    pe.wait_ge(vb_split, l * HEADS + h + 1 + 1)
                    for j in (3, 2, 1, 0):
                        pe.wait_ge(attn_ready, l * 32 + h * 4 + (NC - j))
                        out = ps[3][:, j * P:S]
                        vh, vl = VH[:, j * P:(j + 1) * P], VL[:, j * P:(j + 1) * P]
                        nc.tensor.matmul(out, vh, ATH[j], start=j == NC - 1, stop=False, skip_group_check=True)
                        nc.tensor.matmul(out, vh, ATL[j], start=False, stop=False, skip_group_check=True)
                        last = nc.tensor.matmul(out, vl, ATH[j], start=False, stop=j == 0, skip_group_check=True)
                    last.then_inc(av_done, 1)

                def scores(h):
                    pe.wait_ge(q_split, l * HEADS + h + 1 + 1)
                    pe.wait_ge(k_split, l * HEADS + h + 1 + 1)
                    for j in (3, 2, 1, 0):
                        mm3(ps[4 + j][:, 0:n_keys(j)], KH[:, j * P:(j + 1) * P], KL[:, j * P:(j + 1) * P],
                            QH[:, j * P:S], QL[:, j * P:S], True, True).then_inc(z_done, 1)

                def head(h, first):
                    unit(l, h, U_HEAD, 0, 0, H)
                    if not first:
                        suffix(h - 1, (3, 2))
                        pe.wait_ge(ao_evac, l * HEADS + h)
                    unit(l, h, U_HEAD, 1, 1, H)
                    if not first:
                        suffix(h - 1, (1, 0))
                    pe.wait_ge(q_evac, l * HEADS + h + 1)
                    unit(l, h, U_HEAD, 2, 0, H)
                    if not first:
                        values(h - 1)
                    scores(h)
                    pe.wait_ge(k_evac, l * HEADS + h + 1)
                    unit(l, h, U_HEAD, 3, 1, A)
                    pe.wait_ge(vb_evac, l * HEADS + h + 1)
                    pe.wait_ge(vb_split, l * HEADS + h + 1)
                    for c in range(NC):
                        last = nc.tensor.transpose(ps[2][:, c * P:(c + 1) * P], T[:, 2, c * P:(c + 1) * P],
                                                   ident[:, :])
                    last.then_inc(vb_tr, 1)

                pe.wait_ge(u_gelu, l * KT + KT)
                pe.wait_ge(a_ready, l * KT + KT + 4)
                head(0, True)
                with pe.Fori(1, HEADS) as h:
                    head(h, False)
                suffix(HEADS - 1, (3, 2, 1, 0))
                values(HEADS - 1)

                with pe.Fori(0, KT // 4) as i:
                    for s in range(4):
                        pe.wait_ge(ga_used, l * KT + i * 4 + (s + 3))
                        unit(l, i, U_GA, s, 4 + s % 2, H)
                pe.wait_ge(ao_evac, l * HEADS + HEADS)
                pe.wait_ge(o_split, l * HEADS + HEADS + 1)
                pe.sem_inc(pe_stage, 1)
                with pe.Fori(0, KT // 2) as i:
                    for s in range(4):
                        pe.wait_ge(merged, l * KT + i * 2 + (s // 2 + 1))
                        unit(l, i, U_GB, s, s, O if s % 2 else H)
                pe.wait_ge(merged, l * KT + KT + 2)
                pe.sem_inc(pe_stage, 1)
                with pe.Fori(0, KT // 4) as i:
                    for s in range(4):
                        pe.wait_ge(wo_acc, l * KT + i * 4 + (s + 1))
                        unit(l, i, U_O, s, 4 + s % 2, A)
                post_sum(2 * l)
                norm_sum(l, 1)

                def quarter(q):
                    with pe.Fori(0, UPQ // 2) as i:
                        for s in range(4):
                            pe.wait_ge(conved, ((l * QUARTERS + q) * UPQ + i * 2) * 2 + (s + 1))
                            unit(l, q * (FQ // 4) + i, U_FFN, s, s, H)
                    pe.wait_ge(g_ready, (l * QUARTERS + q) * UPQ + UPQ + 2)
                    pe.sem_inc(pe_stage, 1)
                    with pe.Fori(0, KT // 4) as i:
                        for s in range(4):
                            pe.wait_ge(dn_added, (l * QUARTERS + q) * KT + i * 4 + (s + 1))
                            unit(l, q * (FQ // 4) + 2 * UPQ // 4 + i, U_FFN, s, 4 + s % 2, O)

                with pe.Fori(0, QUARTERS) as q:
                    quarter(q)
                post_sum(2 * l + 1)


def kernel(**inputs):
    import numpy as np
    import concourse.bacc as bacc
    from concourse.bass_utils import run_bass_kernel_spmd as run

    a = {k: np.asarray(v) for k, v in inputs.items()}
    L = DEPTH

    def units(w):
        l_, k, n = w.shape
        return w.reshape(l_, k // P, P, n // P, P).transpose(0, 3, 2, 1, 4)

    w_in = units(a["w_in"]).reshape(L, -1, P, KT * P)
    u_a, v_a, q, k, v, g_a, g_b = (w_in[:, 8 * i:8 * i + 8] for i in range(7))
    flat = lambda w: units(w).reshape(L, -1, P, KT * P)
    a_out, b_out, w_o, up = flat(a["w_a_out"]), flat(a["w_b_out"]), flat(a["w_o"]), flat(a["w_up"])
    pair = lambda *w: np.stack(w, axis=2).reshape(L, -1, P, KT * P)
    up = pair(up[:, :PAIRS], up[:, PAIRS:])
    parts = [v_a, u_a, pair(q, k, v, a_out), g_a, pair(g_b, b_out), w_o]
    for i in range(QUARTERS):
        parts.append(up[:, 2 * UPQ * i:2 * UPQ * (i + 1)])
        parts.append(flat(a["w_down"][:, i * UPQ * P:(i + 1) * UPQ * P]))
    stream = np.ascontiguousarray(np.concatenate(parts, axis=1)).reshape(L * UNITS, P, KT * P)

    vec = lambda x: x.reshape(L, -1, P)
    cols_h = np.concatenate([vec(a[n]) for n in ("b_ada", "g_pre_mix", "g_post_mix", "g_pre_ffn", "g_post_ffn",
                                                 "g_sgu", "conv_b", "conv_w")], axis=1)
    arrays = {
        "xT": a["x"][0].T.reshape(KT, P, S).transpose(1, 0, 2),
        "cvec": a["c"].reshape(1, D),
        "w_stream": stream,
        "w_ada_rows": a["w_ada"].transpose(0, 2, 1).reshape(L * MODS, P, D),
        "cols_d": cols_h.reshape(L * COLS, P).T,
        "w_sp": a["w_spatial"].transpose(0, 3, 1, 2).reshape(L, P, KT * P),
        "b_sp": a["b_spatial"].reshape(L, KT * P),
    }
    arrays = {k_: np.ascontiguousarray(v_) for k_, v_ in arrays.items()}
    nc = bacc.Bacc("TRN2", target_bir_lowering=False, num_devices=1, dynamic_dma_scratch_size=1024)
    args = [nc.dram_tensor(n, x.shape, mybir.dt.from_np(x.dtype), kind="ExternalInput").ap()
            for n, x in arrays.items()]
    out = nc.dram_tensor("outT", (P, KT, S), F32, kind="ExternalOutput").ap()
    build(nc, *args, out)
    r = run(nc, [arrays], core_ids=[0])
    y = r.results[0]["outT"]
    return y.transpose(1, 0, 2).reshape(D, S).T.reshape(1, S, D)
```

```python
from contextlib import ExitStack

import concourse.bass as bass
from concourse import mybir

F32 = mybir.dt.float32
F32R = mybir.dt.float32r
BF16 = mybir.dt.bfloat16
ALU = mybir.AluOpType
ACT = mybir.ActivationFunctionType

P = 128
D = 1024
S = 512
DEPTH = 2
KT = D // P
NC = S // P
HEADS = 8
DFF = 4 * D
QUARTERS = 4
PAIRS = DFF // P
SCALE = float(P) ** -0.5
EPS = 1e-6

U_V = 0
U_U = U_V + KT
U_HEAD = U_U + KT
U_GA = U_HEAD + 4 * HEADS
U_GB = U_GA + KT
U_O = U_GB + 2 * KT
U_FFN = U_O + KT
UPQ = PAIRS // QUARTERS
FQ = 2 * UPQ + KT
UNITS = U_FFN + QUARTERS * FQ
RING = 4
RAW = 2
AHEAD = 2

C_BADA = 0
C_GPREM = 48
C_GPOSTM = 56
C_GPREF = 64
C_GPOSTF = 72
C_GSGU = 80
C_CB = 88
C_CW = C_CB + 2 * PAIRS
COLS = C_CW + 3 * 2 * PAIRS
SHIFT_M, SCALE_M, GATE_M, SHIFT_F, SCALE_F, GATE_F = (8 * i for i in range(6))
MODS = 48
ADA_FIRST = 16
ADA_IN = MODS - ADA_FIRST
ADA_USES = ADA_IN + 1 + ADA_FIRST


def n_keys(j):
    return S - P * j


def build(nc, xT, cvec, w_stream, w_ada, cols_d, w_sp, b_sp, outT):
    with ExitStack() as ctx:
        def sb(name, shape, dt=F32):
            return ctx.enter_context(nc.sbuf_tensor(name, shape, dt))

        def sem(name):
            return ctx.enter_context(nc.semaphore(name))

        X = sb("X", [P, KT, S])
        HH, HL = sb("HH", [P, KT, S], F32R), sb("HL", [P, KT, S], F32R)
        AH, AL = sb("AH", [P, KT, S], F32R), sb("AL", [P, KT, S], F32R)
        OH, OL = sb("OH", [P, KT, S], F32R), sb("OL", [P, KT, S], F32R)
        M = sb("M", [P, KT, S])
        raw = sb("raw", [P, RAW, D])
        WH, WL = sb("WH", [P, RING, KT, P], F32R), sb("WL", [P, RING, KT, P], F32R)
        SC = sb("SC", [P, 14 * S], F32R)
        T = sb("T", [P, 5, S])
        ada = sb("ada", [P, D])
        cact = sb("cact", [P, D])
        cols = sb("cols", [P, DEPTH * COLS])
        mod = sb("mod", [P, DEPTH * MODS])
        acc = sb("acc", [P, 4])
        coef = sb("coef", [P, 2, KT])
        eps = sb("eps", [P, 1])
        ident = sb("ident", [P, P])
        ones = sb("ones", [P, P])
        tmp_tri = sb("tmp_tri", [P, P])
        ntri, nones = sb("ntri", [P, P], F32R), sb("nones", [P, P], F32R)
        strict, negm = sb("strict", [P, P], BF16), sb("negm", [P, P], BF16)
        stats = sb("stats", [P, NC, 2, 6])
        mv = sb("mv", [P, NC, 2])
        rstd = sb("rstd", [P, NC])

        off = {j: sum(n_keys(i) for i in range(j)) for j in range(NC)}
        SPH = {j: SC[:, off[j]:off[j] + n_keys(j)] for j in range(NC)}
        SPL = {j: SC[:, 1280 + off[j]:1280 + off[j] + n_keys(j)] for j in range(NC)}
        ATH = {j: SPH[0] if j == 0 else SC[:, 2560 + off[j] - S:2560 + off[j] - S + n_keys(j)] for j in range(NC)}
        ATL = {j: SPL[0] if j == 0 else SC[:, 3328 + off[j] - S:3328 + off[j] - S + n_keys(j)] for j in range(NC)}
        QH, QL, KH, KL, VH, VL = (SC[:, 4096 + S * i:4096 + S * (i + 1)] for i in range(6))
        WSH, WSL = SC[:, 0:D], SC[:, D:2 * D]
        M_tok = M[:, :, :].rearrange("p m t -> p (m t)").rearrange("p (c d) -> p c d", c=NC)
        ADA0 = [T[:, 0:2].rearrange("p a b -> p (a b)"), T[:, 3:5].rearrange("p a b -> p (a b)"), ada[:, :]]
        GA_BANKS = (0, 1, 2, 4)
        GB_BANKS = (5, 6, 7, 3)

        ps = [ctx.enter_context(nc.psum_tensor(f"ps{i}", [P, S], F32)) for i in range(8)]

        w_landed = [sem(f"w_landed{i}") for i in range(RAW)]
        w_hi, w_split, unit_done = sem("w_hi"), sem("w_split"), sem("unit_done")
        x_landed, cols_landed, c_landed = sem("x_landed"), sem("cols_landed"), sem("c_landed")
        ada_landed, ada_used, ada_bias = sem("ada_landed"), sem("ada_used"), sem("ada_bias")
        ada0_landed = [sem(f"ada0_landed{i}") for i in range(3)]
        c_ready = sem("c_ready")
        bsp_landed, ws_landed = sem("bsp_landed"), sem("ws_landed")
        pool_consts, dve_consts = sem("pool_consts"), sem("dve_consts")
        ws_split = sem("ws_split")
        coef_ready = sem("coef_ready")
        xsq, xsum, xroot, xnorm, h_hi, h_ready = (sem(n) for n in ("xsq", "xsum", "xroot", "xnorm", "h_hi", "h_ready"))
        y_sumsq, y_sum, y_root, x_new = (sem(n) for n in ("y_sumsq", "y_sum", "y_root", "x_new"))
        v_gelu, v_tr, v_copied = sem("v_gelu"), sem("v_tr"), sem("v_copied")
        ln_var, ln_root, vn_ready = sem("ln_var"), sem("ln_root"), sem("vn_ready")
        u_gelu, f_done, a_ready = sem("u_gelu"), sem("f_done"), sem("a_ready")
        q_evac, k_evac, vb_evac, ao_evac = sem("q_evac"), sem("k_evac"), sem("vb_evac"), sem("ao_evac")
        q_split, k_split, vb_tr, vb_split = sem("q_split"), sem("k_split"), sem("vb_tr"), sem("vb_split")
        z_done, ln1p, sp_ready, sfx = sem("z_done"), sem("ln1p"), sem("sp_ready"), sem("sfx")
        arg_masked, attn32, attn_ready = sem("arg_masked"), sem("attn32"), sem("attn_ready")
        av_done, o_split = sem("av_done"), sem("o_split")
        ga_sig, ga_used = sem("ga_sig"), sem("ga_used")
        gb_sig, merged = sem("gb_sig"), sem("merged")
        wo_sq, wo_evac, wo_acc = sem("wo_sq"), sem("wo_evac"), sem("wo_acc")
        tap2, conved, gelued, g_ready = sem("tap2"), sem("conved"), sem("gelued"), sem("g_ready")
        dn_added, dn_sq, dn_acc = sem("dn_added"), sem("dn_sq"), sem("dn_acc")
        out_landed = sem("out_landed")
        act_stage, dve_stage, pe_stage = sem("act_stage"), sem("dve_stage"), sem("pe_stage")

        block = ctx.enter_context(nc.Block())

        def next_layer(l, size, k):
            return nc.s_assert_within(l * size + k + size, size, DEPTH * size - 1,
                                      skip_runtime_bounds_check_because="only where l + 1 is a layer")

        def col(l, c):
            return cols[:, bass.ds(l * COLS + c, 1)]

        @block.sync
        def _(sp):
            sp.dma_start(X[:, :, :], xT).then_inc(x_landed, 16)
            for k in range(ADA_FIRST):
                if k >= 3:
                    sp.wait_ge(ada_bias, k - 2)
                sp.dma_start(ADA0[k % 3], w_ada[k]).then_inc(ada0_landed[k % 3], 16)
                if k == 8:
                    for n in range(RAW):
                        sp.dma_start(raw[:, n], w_stream[n]).then_inc(w_landed[n], 16)
            with sp.Fori(0, (DEPTH * UNITS - RAW) // RAW) as i:
                for s in range(RAW):
                    sp.wait_ge(w_split, i * RAW + (s + 1))
                    sp.dma_start(raw[:, s], w_stream[bass.ds(i * RAW + (s + RAW), 1)].rearrange("o p n -> (o p) n")
                                 ).then_inc(w_landed[s], 16)
            sp.wait_ge(x_new, (DEPTH * 2 + 1) * KT)
            sp.dma_start(outT, X[:, :, :]).then_inc(out_landed, 16)
            sp.wait_ge(out_landed, 16)

        @block.gpsimd
        def _(pool):
            nc.gpsimd.memset(ones[:, :], 1.0).then_inc(pool_consts, 1)
            pool.wait_ge(pool_consts, 1)
            nc.gpsimd.affine_select(out=ident[:, :], in_=ones[:, :], pattern=[[-1, P]], compare_op=ALU.is_equal,
                                    fill=0.0, base=0, channel_multiplier=1)
            nc.gpsimd.affine_select(out=tmp_tri[:, :], in_=ones[:, :], pattern=[[-1, P]], compare_op=ALU.is_ge,
                                    fill=0.0, base=0, channel_multiplier=1).then_inc(pool_consts, 1)
            with pool.Fori(0, DEPTH * UNITS // RING) as i:
                for s in range(RING):
                    pool.wait_ge(w_hi, i * RING + (s + 1))
                    nc.gpsimd.tensor_tensor(WL[:, s].rearrange("p k n -> p (k n)"), raw[:, s % RAW],
                                            WH[:, s].rearrange("p k n -> p (k n)").bitcast(F32),
                                            ALU.subtract).then_inc(w_split, 1)

        @block.scalar
        def _(act):
            def split(l, n, s):
                act.wait_ge(w_landed[s % RAW], (l * (UNITS // 2) + n // 2 + 1) * 16 if isinstance(n, int)
                            else (l * (UNITS // 2) + n[0] * 2 + (n[1] // 2 + 1)) * 16)
                act.wait_ge(unit_done, l * UNITS + n + 1 if isinstance(n, int)
                            else l * UNITS + n[0] * 4 + (n[1] + 1))
                nc.scalar.activation(WH[:, s].rearrange("p k n -> p (k n)"), raw[:, s % RAW],
                                     ACT.Copy).then_inc(w_hi, 1)

            def ahead(l, i, base, s):
                split(l, (i, base + s + AHEAD), (s + AHEAD) % RING)

            def ready(l, i, base, s):
                act.wait_ge(unit_done, l * UNITS + i * 4 + (base + s + 1 + RING))

            def load_ada(l, j):
                act.wait_ge(ada_used, l * ADA_USES + j + 2)
                act.dma_start(ada[:, :], w_ada[bass.ds(l * MODS + (j + ADA_FIRST), 1)].rearrange("o p n -> (o p) n")
                              ).then_inc(ada_landed, 16)

            def squares(l, which):
                n = 2 * l + which
                for m in range(KT):
                    act.wait_ge(x_new, n * KT + m + 1)
                    nc.scalar.activation(M[:, m], X[:, m], ACT.Square).then_inc(xsq, 1)
                act.wait_ge(xsum, n + 1)
                nc.scalar.activation(ps[7][:, :], ps[7][:, :], ACT.Sqrt, bias=eps[:, 0:1], scale=1.0 / D
                                     ).then_inc(xroot, 1)

            def shifted(l, which):
                n = 2 * l + which
                shift = SHIFT_F if which else SHIFT_M
                for m in range(KT):
                    act.wait_ge(xnorm, n * KT + m + 1)
                    nc.scalar.activation(HH[:, m], M[:, m], ACT.Identity,
                                         bias=mod[:, bass.ds(l * MODS + shift + m, 1)]).then_inc(h_hi, 1)

            def post_root(n):
                act.wait_ge(y_sum, n + 1)
                nc.scalar.activation(ps[6][:, :], ps[6][:, :], ACT.Sqrt, bias=eps[:, 0:1], scale=1.0 / D
                                     ).then_inc(y_root, 1)

            act.sem_inc(wo_evac, 2)
            act.dma_start(cact[:, :], cvec.to_broadcast([P, D])).then_inc(c_landed, 16)
            act.dma_start(cols[:, :], cols_d).then_inc(cols_landed, 16)
            act.wait_ge(c_landed, 16)
            nc.scalar.activation(cact[:, :], cact[:, :], ACT.Silu).then_inc(c_ready, 1)
            act.wait_ge(dve_consts, 1)
            act.sem_inc(act_stage, 1)
            with act.Fori(0, DEPTH) as l:
                squares(l, 0)
                act.wait_ge(ada_used, l * ADA_USES + 1)
                act.dma_start(ada[:, :], b_sp[bass.ds(l, 1)].to_broadcast([P, D])).then_inc(bsp_landed, 16)
                act.dma_start(T[:, 3:5], w_sp[bass.ds(l, 1)].rearrange("o p n -> (o p) n").rearrange(
                    "p (a b) -> p a b", a=2)).then_inc(ws_landed, 16)
                for n in range(AHEAD):
                    split(l, n, n)
                shifted(l, 0)

                with act.Fori(0, KT // 4) as i:
                    for s in range(4):
                        ahead(l, i, U_V, s)
                        ready(l, i, U_V, s)
                        act.wait_ge(v_tr, l * KT + i * 4 + (s + 1))
                        if s == 3:
                            act.wait_ge(ws_split, l + 1)
                        nc.scalar.activation(T[:, s], ps[s % 2][:, :], ACT.Gelu).then_inc(v_gelu, 1)
                act.wait_ge(ln_var, l + 1)
                nc.scalar.activation(rstd[:, :], mv[:, :, 1], ACT.Sqrt, bias=eps[:, 0:1]).then_inc(ln_root, 1)
                with act.Fori(0, KT // 4) as i:
                    for s in range(4):
                        ahead(l, i, U_U, s)
                        ready(l, i, U_U, s)
                        act.wait_ge(v_tr, l * KT + (s + 1 + KT))
                        act.wait_ge(a_ready, l * KT + i * 4 + (s + 1))
                        nc.scalar.activation(T[:, s], ps[s][:, :], ACT.Gelu).then_inc(u_gelu, 1)

                nc.scalar.preload_act_table_set("natural_log_exp_and_others")

                def exps(h, js):
                    for j in js:
                        act.wait_ge(arg_masked, l * 32 + h * 4 + (NC - j))
                        if j < 2:
                            act.wait_ge(attn_ready, l * 32 + h * 4 + (NC - j - 2))
                        nc.scalar.activation(T[:, 3 + j % 2, 0:n_keys(j)], ps[4 + j][:, 0:n_keys(j)],
                                             ACT.Exp).then_inc(attn32, 1)

                def head(h, first):
                    base = U_HEAD
                    ahead(l, h, base, 0)
                    ready(l, h, base, 0)
                    act.wait_ge(q_split, l * HEADS + h + 1)
                    nc.scalar.activation(T[:, 0], ps[0][:, :], ACT.Copy, scale=SCALE).then_inc(q_evac, 1)
                    load_ada(l, h * 2)
                    if not first:
                        exps(h - 1, (3, 2))
                    ahead(l, h, base, 1)
                    ready(l, h, base, 1)
                    act.wait_ge(k_split, l * HEADS + h + 1)
                    nc.scalar.activation(T[:, 1], ps[1][:, :], ACT.Copy).then_inc(k_evac, 1)
                    if not first:
                        exps(h - 1, (1, 0))
                    ahead(l, h, base, 2)
                    ready(l, h, base, 2)
                    act.wait_ge(vb_tr, l * HEADS + h + 1)
                    nc.scalar.activation(T[:, 2], ps[0][:, :], ACT.Copy).then_inc(vb_evac, 1)
                    ahead(l, h, base, 3)
                    load_ada(l, h * 2 + 1)
                    for j in (3, 2, 1, 0):
                        n = n_keys(j)
                        e = T[:, 3 + j % 2, 0:n]
                        act.wait_ge(z_done, l * 32 + h * 4 + (NC - j))
                        if j < 2:
                            act.wait_ge(sp_ready, l * 32 + h * 4 + (NC - j - 2))
                        elif not first:
                            act.wait_ge(attn_ready, l * 32 + h * 4)
                        nc.scalar.activation(e, ps[4 + j][:, 0:n], ACT.Abs)
                        act.drain()
                        nc.scalar.activation(e, e, ACT.Exp, scale=-1.0)
                        act.drain()
                        nc.scalar.activation(e, e, ACT.Ln, bias=1.0).then_inc(ln1p, 1)
                    ready(l, h, base, 3)
                    nc.scalar.activation(M[:, bass.ds(h, 1)].rearrange("p o t -> p (o t)"), ps[1][:, :],
                                         ACT.Copy).then_inc(ao_evac, 1)

                act.wait_ge(a_ready, l * KT + (KT + 2))
                head(0, True)
                with act.Fori(1, HEADS) as h:
                    head(h, False)
                for u in range(KT):
                    ahead(l, u // 4, U_GA, u % 4)
                    ready(l, u // 4, U_GA, u % 4)
                    if u == 0:
                        exps(HEADS - 1, (3, 2))
                    if u == 1:
                        exps(HEADS - 1, (1, 0))
                    if u >= 2:
                        for v in (0, 1, 2) if u == 2 else (u,):
                            if v >= 4:
                                act.wait_ge(ga_used, l * KT + v - 4 + 1 + 4)
                            if v == 3:
                                act.wait_ge(attn_ready, l * 32 + 32)
                            nc.scalar.activation(T[:, v % 4], ps[GA_BANKS[v % 4]][:, :], ACT.Sigmoid
                                                 ).then_inc(ga_sig, 1)
                act.wait_ge(ga_used, l * KT + (KT + 4))
                act.sem_inc(act_stage, 1)
                with act.Fori(0, KT // 2) as i:
                    for s in range(4):
                        ahead(l, i, U_GB, s)
                        if s % 2 == 0:
                            ready(l, i, U_GB, s)
                            act.wait_ge(merged, l * KT + i * 2 + (s // 2 + 1))
                            nc.scalar.activation(T[:, s], ps[GB_BANKS[s]][:, :], ACT.Sigmoid).then_inc(gb_sig, 1)
                        load_ada(l, i * 4 + (2 * HEADS + s))
                nc.scalar.preload_act_table(ACT.Sqrt)
                act.wait_ge(merged, l * KT + (KT + 2))
                act.sem_inc(act_stage, 1)
                with act.Fori(0, KT // 4) as i:
                    for s in range(4):
                        ahead(l, i, U_O, s)
                        ready(l, i, U_O, s)
                        act.wait_ge(wo_acc, l * KT + i * 4 + (s + 1))
                        nc.scalar.activation(T[:, s % 2], ps[s % 2][:, :], ACT.Square).then_inc(wo_sq, 1)
                        nc.scalar.activation(M[:, bass.ds(i * 4 + s, 1)].rearrange("p o t -> p (o t)"),
                                             ps[s % 2][:, :], ACT.Copy).then_inc(wo_evac, 1)
                post_root(2 * l)
                squares(l, 1)
                shifted(l, 1)

                def tap(l, q, i, s):
                    tile = q * UPQ + i * 2 + (s // 2 + PAIRS * (s % 2))
                    act.wait_ge(g_ready, (l * QUARTERS + q) * UPQ + i * 2 + (s // 2 + 1))
                    nc.scalar.activation(T[:, s], ps[s][:, :], ACT.Identity, scale=col(l, tile + (C_CW + 4 * PAIRS)),
                                         bias=col(l, tile + C_CB)).then_inc(tap2, 1)

                def quarter(q, last):
                    with act.Fori(0, UPQ // 2) as i:
                        for s in range(4):
                            n = q * (FQ // 4) + i
                            ahead(l, n, U_FFN, s)
                            ready(l, n, U_FFN, s)
                            tap(l, q, i, s)
                            if s == 0:
                                with act.If(l < DEPTH - 1):
                                    k = q * (UPQ // 2) + i
                                    act.wait_ge(ada_used, l * ADA_USES + k + (ADA_IN + 2))
                                    act.dma_start(ada[:, :], w_ada[bass.ds(next_layer(l, MODS, k), 1)].rearrange(
                                        "o p n -> (o p) n")).then_inc(ada_landed, 16)
                            if s % 2:
                                act.wait_ge(conved, ((l * QUARTERS + q) * UPQ + i * 2) * 2 + (s + 4))
                                nc.scalar.activation(T[:, s - 1], T[:, s - 1], ACT.Gelu_apprx_tanh
                                                     ).then_inc(gelued, 1)
                    if last:
                        nc.scalar.preload_act_table(ACT.Sqrt)
                    for i in range(KT // 4):
                        for s in range(4):
                            n = q * (FQ // 4) + (2 * UPQ // 4 + i)
                            if not last or 4 * i + s + AHEAD < KT:
                                ahead(l, n, U_FFN, s)
                            if last:
                                m = 4 * i + s
                                act.wait_ge(dn_added, l * KT * QUARTERS + (QUARTERS - 1) * KT + m + 1 + 2)
                                act.wait_ge(dn_acc, l * KT + m + 1)
                                nc.scalar.activation(T[:, s % 2], M[:, m], ACT.Square).then_inc(dn_sq, 1)

                act.wait_ge(g_ready, l * PAIRS + 2)
                act.sem_inc(act_stage, 1)
                with act.Fori(0, QUARTERS - 1) as q:
                    quarter(q, False)
                act.wait_ge(g_ready, (l + 1) * PAIRS + 2 - UPQ)
                quarter(QUARTERS - 1, True)
                post_root(2 * l + 1)

        @block.vector
        def _(dve):
            def ready(l, i, base, s):
                dve.wait_ge(unit_done, l * UNITS + i * 4 + (base + s + 1 + RING))

            def hi_lo(hi, lo, src, done):
                nc.vector.tensor_copy(hi, src)
                dve.drain()
                return nc.vector.tensor_tensor(lo, src, hi.bitcast(F32), ALU.subtract).then_inc(done, 1)

            def ada_unit(l, j):
                dve.wait_ge(ada_landed, l * MODS * 16 + (j + 1) * 16)
                nc.vector.tensor_tensor_reduce(out=ada[:, :], in0=ada[:, :], in1=cact[:, :], scale=1.0, scalar=0.0,
                                               op0=ALU.mult, op1=ALU.add, accum_out=acc[:, 0:1]).then_inc(ada_used, 1)
                dve.drain()
                nc.vector.tensor_tensor(mod[:, bass.ds(l * MODS + j + ADA_FIRST, 1)], acc[:, 0:1],
                                        col(l, j + (C_BADA + ADA_FIRST)), ALU.add)
                dve.drain()

            def modulation(l, which):
                sc, g = (SCALE_F, C_GPREF) if which else (SCALE_M, C_GPREM)
                nc.vector.scalar_tensor_tensor(out=coef[:, 0], in0=mod[:, bass.ds(l * MODS + sc, KT)], scalar=1.0,
                                               in1=cols[:, bass.ds(l * COLS + g, KT)], op0=ALU.add,
                                               op1=ALU.mult).then_inc(coef_ready, 1)

            def norm(l, which):
                n = 2 * l + which
                shift = SHIFT_F if which else SHIFT_M

                def low(m):
                    dve.wait_ge(h_hi, n * KT + m + 1)
                    nc.vector.scalar_tensor_tensor(out=HL[:, m], in0=M[:, m],
                                                   scalar=mod[:, bass.ds(l * MODS + shift + m, 1)],
                                                   in1=HH[:, m].bitcast(F32), op0=ALU.add, op1=ALU.subtract
                                                   ).then_inc(h_ready, 1)

                dve.wait_ge(xroot, n + 1)
                nc.vector.reciprocal(ps[7][:, :], ps[7][:, :])
                dve.drain()
                for m in range(KT):
                    nc.vector.scalar_tensor_tensor(out=M[:, m], in0=X[:, m], scalar=coef[:, 0, m:m + 1],
                                                   in1=ps[7][:, :], op0=ALU.mult, op1=ALU.mult).then_inc(xnorm, 1)
                    if m:
                        low(m - 1)
                low(KT - 1)
                dve.drain()

            def post(l, which):
                gate, g = (GATE_F, C_GPOSTF) if which else (GATE_M, C_GPOSTM)
                nc.vector.scalar_tensor_tensor(out=coef[:, 1], in0=mod[:, bass.ds(l * MODS + gate, KT)], scalar=1.0,
                                               in1=cols[:, bass.ds(l * COLS + g, KT)], op0=ALU.add, op1=ALU.mult)
                dve.wait_ge(y_root, 2 * l + which + 1)
                nc.vector.reciprocal(ps[6][:, :], ps[6][:, :])
                dve.drain()
                for m in range(KT + 1):
                    if m < KT:
                        nc.vector.scalar_tensor_tensor(out=M[:, m], in0=M[:, m], scalar=coef[:, 1, m:m + 1],
                                                       in1=ps[6][:, :], op0=ALU.mult, op1=ALU.mult)
                    if m:
                        nc.vector.tensor_tensor(X[:, m - 1], X[:, m - 1], M[:, m - 1], ALU.add).then_inc(x_new, 1)
                    dve.drain()

            dve.wait_ge(pool_consts, 2)
            nc.vector.memset(eps[:, :], EPS)
            nc.vector.tensor_scalar(ntri[:, :], tmp_tri[:, :], -1.0, None, ALU.mult)
            nc.vector.tensor_scalar(nones[:, :], ones[:, :], -1.0, None, ALU.mult)
            nc.vector.tensor_scalar(strict[:, :], tmp_tri[:, :], -1.0, 1.0, ALU.mult, ALU.add)
            nc.vector.tensor_scalar(negm[:, :], tmp_tri[:, :], -1e30, None, ALU.mult).then_inc(dve_consts, 1)
            dve.drain()
            dve.wait_ge(cols_landed, 16)
            dve.wait_ge(x_landed, 16)
            dve.sem_inc(x_new, KT)
            dve.wait_ge(c_ready, 1)
            for k in range(ADA_FIRST):
                dve.wait_ge(ada0_landed[k % 3], 16 * (k // 3 + 1))
                nc.vector.tensor_tensor_reduce(out=ADA0[k % 3], in0=ADA0[k % 3], in1=cact[:, :], scale=1.0,
                                               scalar=0.0, op0=ALU.mult, op1=ALU.add,
                                               accum_out=acc[:, 0:1])
                dve.drain()
                nc.vector.tensor_tensor(mod[:, k:k + 1], acc[:, 0:1], cols[:, C_BADA + k:C_BADA + k + 1],
                                        ALU.add).then_inc(ada_bias, 1)
                dve.drain()
            dve.sem_inc(ada_used, 1)
            dve.sem_inc(v_copied, 2)
            dve.sem_inc(a_ready, 4)
            dve.sem_inc(q_split, 1)
            dve.sem_inc(k_split, 1)
            dve.sem_inc(o_split, 1)
            dve.sem_inc(vb_split, 1)
            dve.sem_inc(ga_used, 4)
            dve.sem_inc(merged, 2)
            dve.sem_inc(wo_acc, 2)
            dve.sem_inc(conved, 4)
            dve.sem_inc(g_ready, 2)
            dve.sem_inc(dn_added, 2)
            dve.sem_inc(dn_acc, 2)

            with dve.Fori(0, DEPTH) as l:
                modulation(l, 0)
                dve.drain()
                norm(l, 0)
                dve.wait_ge(ws_landed, l * 16 + 16)
                nc.vector.tensor_tensor(tmp_tri[:, :], strict[:, :], ident[:, :], ALU.add)
                dve.drain()
                ws = T[:, 3:5].rearrange("p a b -> p (a b)").rearrange("p (g t) -> p g t", g=KT)
                nc.vector.tensor_tensor(ws, ws, tmp_tri[:, :].unsqueeze(1).to_broadcast([P, KT, P]), ALU.mult)
                dve.drain()
                hi_lo(WSH, WSL, T[:, 3:5].rearrange("p a b -> p (a b)"), ws_split)
                dve.drain()

                with dve.Fori(0, KT // 4) as i:
                    for s in range(4):
                        dve.wait_ge(v_tr, l * KT + i * 4 + (s + 1 + 4))
                        nc.vector.tensor_copy(M_tok[:, :, bass.ds((i * 4 + s) * P, P)],
                                              ps[2 + s % 2][:, :].rearrange("p (c d) -> p c d", c=NC)
                                              ).then_inc(v_copied, 1)
                dve.drain()
                for c in range(NC):
                    for half in range(2):
                        nc.vector.bn_stats(stats[:, c, half], M_tok[:, c, half * S:(half + 1) * S])
                dve.drain()
                for c in range(NC):
                    ins = nc.vector.bn_aggr(mv[:, c], stats[:, c])
                ins.then_inc(ln_var, 1)
                dve.wait_ge(ln_root, l + 1)
                nc.vector.reciprocal(rstd[:, :], rstd[:, :])
                dve.drain()
                for c in range(NC):
                    nc.vector.tensor_scalar(M_tok[:, c], M_tok[:, c], mv[:, c, 0:1], rstd[:, c:c + 1], ALU.subtract,
                                            ALU.mult)
                dve.drain()
                for c in range(NC):
                    src = M_tok[:, c].rearrange("p (g d) -> p g d", g=KT)
                    nc.vector.tensor_copy(AH[:, :, c * P:(c + 1) * P], src)
                dve.drain()
                for c in range(NC):
                    src = M_tok[:, c].rearrange("p (g d) -> p g d", g=KT)
                    nc.vector.tensor_tensor(AL[:, :, c * P:(c + 1) * P], src,
                                            AH[:, :, c * P:(c + 1) * P].bitcast(F32),
                                            ALU.subtract).then_inc(vn_ready, 1)

                dve.wait_ge(bsp_landed, l * 16 + 16)
                dve.sem_inc(dve_stage, 1)
                with dve.Fori(0, KT // 4) as i:
                    for s in range(4):
                        g = i * 4 + s
                        dve.wait_ge(f_done, l * KT + g + 1)
                        dve.wait_ge(u_gelu, l * KT + g + 1)
                        f = ps[4 + s % 2][:, :]
                        bias = ada[:, bass.ds(g * P, P)].unsqueeze(1).to_broadcast([P, NC, P])
                        fc = f.rearrange("p (c t) -> p c t", c=NC)
                        nc.vector.scalar_tensor_tensor(out=fc, in0=fc, scalar=col(l, g + C_GSGU), in1=bias,
                                                       op0=ALU.mult, op1=ALU.add)
                        dve.drain()
                        nc.vector.tensor_tensor(T[:, s], T[:, s], f, ALU.mult)
                        dve.drain()
                        hi_lo(AH[:, bass.ds(g, 1)].rearrange("p o t -> p (o t)"),
                              AL[:, bass.ds(g, 1)].rearrange("p o t -> p (o t)"), T[:, s], a_ready)
                dve.drain().then_inc(ada_used, 1)

                def attn(h, js):
                    for j in js:
                        n = n_keys(j)
                        dve.wait_ge(sfx, l * 32 + h * 4 + (NC - j))
                        nc.vector.tensor_tensor(ps[4 + j][:, 0:P], ps[4 + j][:, 0:P], negm[:, :],
                                                ALU.add).then_inc(arg_masked, 1)
                        dve.wait_ge(attn32, l * 32 + h * 4 + (NC - j))
                        hi_lo(ATH[j], ATL[j], T[:, 3 + j % 2, 0:n], attn_ready)

                def out_split(h):
                    dve.wait_ge(av_done, l * HEADS + h + 1)
                    hi_lo(OH[:, bass.ds(h, 1)].rearrange("p o t -> p (o t)"),
                          OL[:, bass.ds(h, 1)].rearrange("p o t -> p (o t)"), ps[3][:, :], o_split)

                def head(h, first):
                    dve.wait_ge(q_evac, l * HEADS + h + 1)
                    hi_lo(QH, QL, T[:, 0], q_split)
                    if not first:
                        attn(h - 1, (3, 2))
                    dve.wait_ge(k_evac, l * HEADS + h + 1)
                    hi_lo(KH, KL, T[:, 1], k_split)
                    if not first:
                        attn(h - 1, (1, 0))
                    ada_unit(l, h * 2)
                    if not first:
                        out_split(h - 1)
                    for j in (3, 2, 1, 0):
                        n = n_keys(j)
                        e = T[:, 3 + j % 2, 0:n]
                        dve.wait_ge(ln1p, l * 32 + h * 4 + (NC - j))
                        nc.vector.scalar_tensor_tensor(out=e, in0=ps[4 + j][:, 0:n], scalar=0.0, in1=e, op0=ALU.max,
                                                       op1=ALU.add)
                        dve.drain()
                        nc.vector.tensor_tensor(e[:, 0:P], e[:, 0:P], strict[:, :], ALU.mult)
                        dve.drain()
                        hi_lo(SPH[j], SPL[j], e, sp_ready)
                    dve.wait_ge(vb_tr, l * HEADS + h + 1 + 1)
                    hi_lo(VH, VL, ps[2][:, :], vb_split)
                    ada_unit(l, h * 2 + 1)

                head(0, True)
                with dve.Fori(1, HEADS) as h:
                    head(h, False)
                attn(HEADS - 1, (3, 2, 1, 0))
                out_split(HEADS - 1)

                dve.wait_ge(ao_evac, l * HEADS + HEADS)
                dve.sem_inc(dve_stage, 1)
                with dve.Fori(0, KT // 4) as i:
                    for s in range(4):
                        m = M[:, bass.ds(i * 4 + s, 1)].rearrange("p o t -> p (o t)")
                        dve.wait_ge(ga_sig, l * KT + i * 4 + (s + 1))
                        nc.vector.tensor_tensor(m, m, T[:, s], ALU.mult).then_inc(ga_used, 1)
                dve.drain()
                with dve.Fori(0, KT // 2) as i:
                    for s in (1, 3):
                        g = i * 2 + s // 2
                        dve.wait_ge(gb_sig, l * KT + g + 1)
                        ready(l, i, U_GB, s)
                        nc.vector.tensor_tensor(T[:, s - 1], T[:, s - 1], ps[GB_BANKS[s]][:, :], ALU.mult)
                        dve.drain()
                        nc.vector.tensor_tensor(T[:, s - 1], T[:, s - 1],
                                                M[:, bass.ds(g, 1)].rearrange("p o t -> p (o t)"), ALU.add)
                        dve.drain()
                        hi_lo(AH[:, bass.ds(g, 1)].rearrange("p o t -> p (o t)"),
                              AL[:, bass.ds(g, 1)].rearrange("p o t -> p (o t)"), T[:, s - 1], merged)
                        ada_unit(l, i * 4 + (2 * HEADS + s - 1))
                        ada_unit(l, i * 4 + (2 * HEADS + s))
                modulation(l, 1)
                nc.vector.memset(T[:, 2], 0.0)
                dve.drain()
                with dve.Fori(0, KT // 4) as i:
                    for s in range(4):
                        dve.wait_ge(wo_sq, l * KT + i * 4 + (s + 1))
                        nc.vector.tensor_tensor(T[:, 2], T[:, 2], T[:, s % 2], ALU.add).then_inc(wo_acc, 1)
                        dve.drain()
                dve.drain().then_inc(y_sumsq, 1)
                dve.wait_ge(wo_evac, l * KT + KT + 2)
                post(l, 0)
                norm(l, 1)

                nc.vector.memset(M[:, :, :], 0.0)

                def quarter(q, last):
                    with dve.Fori(0, UPQ // 2) as i:
                        for s in range(4):
                            tile = q * UPQ + i * 2 + (s // 2 + PAIRS * (s % 2))
                            dve.wait_ge(tap2, ((l * QUARTERS + q) * UPQ + i * 2) * 2 + (s + 1))
                            nc.vector.scalar_tensor_tensor(out=T[:, s, 1:S], in0=ps[s][:, 0:S - 1],
                                                           scalar=col(l, tile + (C_CW + 2 * PAIRS)), in1=T[:, s, 1:S],
                                                           op0=ALU.mult, op1=ALU.add)
                            dve.drain()
                            nc.vector.scalar_tensor_tensor(out=T[:, s, 2:S], in0=ps[s][:, 0:S - 2],
                                                           scalar=col(l, tile + C_CW), in1=T[:, s, 2:S],
                                                           op0=ALU.mult, op1=ALU.add).then_inc(conved, 1)
                            if s % 2:
                                g = i * 2 + s // 2
                                dve.drain()
                                dve.wait_ge(gelued, (l * QUARTERS + q) * UPQ + g + 1)
                                nc.vector.tensor_tensor(T[:, s], T[:, s - 1], T[:, s], ALU.mult)
                                dve.drain()
                                hi_lo(OH[:, bass.ds(g, 1)].rearrange("p o t -> p (o t)"),
                                      OL[:, bass.ds(g, 1)].rearrange("p o t -> p (o t)"), T[:, s], g_ready)
                            if s == 3:
                                with dve.If(l < DEPTH - 1):
                                    k = q * (UPQ // 2) + i
                                    dve.wait_ge(ada_landed, (l * MODS + k + (ADA_IN + 1)) * 16)
                                    nc.vector.tensor_tensor_reduce(
                                        out=ada[:, :], in0=ada[:, :], in1=cact[:, :], scale=1.0, scalar=0.0,
                                        op0=ALU.mult, op1=ALU.add, accum_out=acc[:, 0:1]).then_inc(ada_used, 1)
                                    dve.drain()
                                    nc.vector.tensor_tensor(mod[:, bass.ds(next_layer(l, MODS, k), 1)], acc[:, 0:1],
                                                            cols[:, bass.ds(next_layer(l, COLS, k + C_BADA), 1)], ALU.add)
                                    dve.drain()
                    if last:
                        nc.vector.memset(T[:, 2], 0.0)
                    dve.drain()
                    for m in range(KT):
                        n = q * (FQ // 4) + (2 * UPQ // 4 + m // 4)
                        ready(l, n, U_FFN, m % 4)
                        nc.vector.tensor_tensor(M[:, m], M[:, m], ps[4 + m % 2][:, :], ALU.add).then_inc(dn_added, 1)
                        if last:
                            dve.wait_ge(dn_sq, l * KT + m + 1)
                            nc.vector.tensor_tensor(T[:, 2], T[:, 2], T[:, m % 2], ALU.add).then_inc(dn_acc, 1)
                            dve.drain()
                    dve.drain()

                with dve.Fori(0, QUARTERS - 1) as q:
                    quarter(q, False)
                quarter(QUARTERS - 1, True)
                dve.drain().then_inc(y_sumsq, 1)
                post(l, 1)

        @block.tensor
        def _(pe):
            def mm3(out, wh, wl, xh, xl, start, stop):
                nc.tensor.matmul(out, wh, xh, start=start, stop=False)
                nc.tensor.matmul(out, wh, xl, start=False, stop=False)
                return nc.tensor.matmul(out, wl, xh, start=False, stop=stop)

            def unit(l, i, base, s, bank, src, tiles=None):
                pe.wait_ge(w_split, l * UNITS + i * 4 + (base + s + 1))
                for k in range(KT):
                    if tiles:
                        pe.wait_ge(tiles[0], tiles[1] + (k + 1))
                    last = mm3(ps[bank][:, :], WH[:, s, k], WL[:, s, k], src[0][:, k], src[1][:, k],
                               k == 0, k == KT - 1)
                last.then_inc(unit_done, 1)

            H, A, O = (HH, HL), (AH, AL), (OH, OL)

            def norm_sum(l, which):
                n = 2 * l + which
                for m in range(KT):
                    pe.wait_ge(xsq, n * KT + m + 1)
                    last = nc.tensor.matmul(ps[7][:, :], ones[:, :], M[:, m], start=m == 0, stop=m == KT - 1)
                last.then_inc(xsum, 1)
                pe.sem_inc(pe_stage, 1)

            def post_sum(n):
                pe.wait_ge(y_sumsq, n + 1)
                nc.tensor.matmul(ps[6][:, :], ones[:, :], T[:, 2], start=True, stop=True).then_inc(y_sum, 1)

            pe.sem_inc(unit_done, RING)
            pe.sem_inc(v_tr, 4)
            pe.sem_inc(vb_tr, 1)
            pe.wait_ge(dve_consts, 1)
            pe.sem_inc(pe_stage, 1)
            with pe.Fori(0, DEPTH) as l:
                norm_sum(l, 0)

                def v_transpose(i, s):
                    pe.wait_ge(v_gelu, l * KT + i * 4 + (s + 1))
                    pe.wait_ge(v_copied, l * KT + i * 4 + (s + 1))
                    for c in range(NC):
                        last = nc.tensor.transpose(ps[2 + s % 2][:, c * P:(c + 1) * P], T[:, s, c * P:(c + 1) * P],
                                                   ident[:, :])
                    last.then_inc(v_tr, 1)

                with pe.Fori(0, KT // 4) as i:
                    unit(l, i, U_V, 0, 0, H, (h_ready, 2 * l * KT))
                    unit(l, i, U_V, 1, 1, H)
                    v_transpose(i, 0)
                    unit(l, i, U_V, 2, 0, H)
                    v_transpose(i, 1)
                    unit(l, i, U_V, 3, 1, H)
                    v_transpose(i, 2)
                    v_transpose(i, 3)
                def spatial(g):
                    if g >= 2:
                        pe.wait_ge(a_ready, l * KT + g - 1 + 4)
                    for c in range(NC):
                        last = mm3(ps[4 + g % 2][:, c * P:(c + 1) * P], AH[:, g, c * P:(c + 1) * P],
                                   AL[:, g, c * P:(c + 1) * P], WSH[:, g * P:(g + 1) * P],
                                   WSL[:, g * P:(g + 1) * P], True, True)
                    last.then_inc(f_done, 1)

                for u in range(KT):
                    if u == 2:
                        pe.wait_ge(v_copied, l * KT + KT + 2)
                    if u >= 4:
                        pe.wait_ge(u_gelu, l * KT + u - 3)
                    unit(l, u // 4, U_U, u % 4, u % 4, H)
                    if u == 3:
                        pe.wait_ge(vn_ready, l * NC + NC)
                        spatial(0)
                        spatial(1)
                    if u > 3:
                        spatial(u - 2)

                def suffix(h, js):
                    for j in js:
                        pe.wait_ge(sp_ready, l * 32 + h * 4 + (NC - j))
                        for k in range(j, NC):
                            at = (k - j) * P
                            for part in (SPH[k], SPL[k]):
                                last = nc.tensor.matmul(ps[4 + j][:, at:n_keys(j)],
                                                        ntri[:, :] if k == j else nones[:, :], part, start=False,
                                                        stop=True, skip_group_check=True)
                        last.then_inc(sfx, 1)

                def values(h):
                    pe.wait_ge(o_split, l * HEADS + h + 1)
                    pe.wait_ge(vb_split, l * HEADS + h + 1 + 1)
                    for j in (3, 2, 1, 0):
                        pe.wait_ge(attn_ready, l * 32 + h * 4 + (NC - j))
                        out = ps[3][:, j * P:S]
                        vh, vl = VH[:, j * P:(j + 1) * P], VL[:, j * P:(j + 1) * P]
                        nc.tensor.matmul(out, vh, ATH[j], start=j == NC - 1, stop=False, skip_group_check=True)
                        nc.tensor.matmul(out, vh, ATL[j], start=False, stop=False, skip_group_check=True)
                        last = nc.tensor.matmul(out, vl, ATH[j], start=False, stop=j == 0, skip_group_check=True)
                    last.then_inc(av_done, 1)

                def scores(h):
                    pe.wait_ge(q_split, l * HEADS + h + 1 + 1)
                    pe.wait_ge(k_split, l * HEADS + h + 1 + 1)
                    for j in (3, 2, 1, 0):
                        mm3(ps[4 + j][:, 0:n_keys(j)], KH[:, j * P:(j + 1) * P], KL[:, j * P:(j + 1) * P],
                            QH[:, j * P:S], QL[:, j * P:S], True, True).then_inc(z_done, 1)

                def head(h, first):
                    unit(l, h, U_HEAD, 0, 0, H)
                    if first:
                        spatial(6)
                    if not first:
                        suffix(h - 1, (3, 2))
                        pe.wait_ge(ao_evac, l * HEADS + h)
                    unit(l, h, U_HEAD, 1, 1, H)
                    if first:
                        spatial(7)
                    if not first:
                        suffix(h - 1, (1, 0))
                    pe.wait_ge(q_evac, l * HEADS + h + 1)
                    unit(l, h, U_HEAD, 2, 0, H)
                    if first:
                        pe.wait_ge(a_ready, l * KT + KT + 4)
                    else:
                        values(h - 1)
                    scores(h)
                    pe.wait_ge(k_evac, l * HEADS + h + 1)
                    unit(l, h, U_HEAD, 3, 1, A)
                    pe.wait_ge(vb_evac, l * HEADS + h + 1)
                    pe.wait_ge(vb_split, l * HEADS + h + 1)
                    for c in range(NC):
                        last = nc.tensor.transpose(ps[2][:, c * P:(c + 1) * P], T[:, 2, c * P:(c + 1) * P],
                                                   ident[:, :])
                    last.then_inc(vb_tr, 1)

                pe.wait_ge(u_gelu, l * KT + KT - 1)
                head(0, True)
                with pe.Fori(1, HEADS) as h:
                    head(h, False)
                pe.wait_ge(ao_evac, l * HEADS + HEADS)
                for u in range(KT):
                    if u == 2:
                        pe.wait_ge(vb_split, l * HEADS + HEADS + 1)
                    if u >= 4:
                        pe.wait_ge(ga_sig, l * KT + u - 3)
                    unit(l, u // 4, U_GA, u % 4, GA_BANKS[u % 4], H)
                    if u == 0:
                        suffix(HEADS - 1, (3, 2))
                    if u == 1:
                        suffix(HEADS - 1, (1, 0))
                    if u == 2:
                        values(HEADS - 1)
                pe.wait_ge(o_split, l * HEADS + HEADS + 1)
                pe.sem_inc(pe_stage, 1)
                with pe.Fori(0, KT // 2) as i:
                    for s in range(4):
                        pe.wait_ge(merged, l * KT + i * 2 + (s // 2 + 1))
                        unit(l, i, U_GB, s, GB_BANKS[s], O if s % 2 else H)
                with pe.Fori(0, KT // 4) as i:
                    for s in range(4):
                        pe.wait_ge(wo_evac, l * KT + i * 4 + (s + 1))
                        unit(l, i, U_O, s, s % 2, A, None if s else (merged, l * KT + 2))
                post_sum(2 * l)
                norm_sum(l, 1)

                def quarter(q):
                    with pe.Fori(0, UPQ // 2) as i:
                        for s in range(4):
                            pe.wait_ge(conved, ((l * QUARTERS + q) * UPQ + i * 2) * 2 + (s + 1))
                            unit(l, q * (FQ // 4) + i, U_FFN, s, s, H,
                                 None if s else (h_ready, (2 * l + 1) * KT))
                    with pe.Fori(0, KT // 4) as i:
                        for s in range(4):
                            pe.wait_ge(dn_added, (l * QUARTERS + q) * KT + i * 4 + (s + 1))
                            unit(l, q * (FQ // 4) + 2 * UPQ // 4 + i, U_FFN, s, 4 + s % 2, O,
                                 None if s else (g_ready, (l * QUARTERS + q) * UPQ + 2))

                with pe.Fori(0, QUARTERS) as q:
                    quarter(q)
                post_sum(2 * l + 1)


def kernel(**inputs):
    import numpy as np
    import concourse.bacc as bacc
    from concourse.bass_utils import run_bass_kernel_spmd as run

    a = {k: np.asarray(v) for k, v in inputs.items()}
    L = DEPTH

    def units(w):
        l_, k, n = w.shape
        return w.reshape(l_, k // P, P, n // P, P).transpose(0, 3, 2, 1, 4)

    w_in = units(a["w_in"]).reshape(L, -1, P, KT * P)
    u_a, v_a, q, k, v, g_a, g_b = (w_in[:, 8 * i:8 * i + 8] for i in range(7))
    flat = lambda w: units(w).reshape(L, -1, P, KT * P)
    a_out, b_out, w_o, up = flat(a["w_a_out"]), flat(a["w_b_out"]), flat(a["w_o"]), flat(a["w_up"])
    pair = lambda *w: np.stack(w, axis=2).reshape(L, -1, P, KT * P)
    up = pair(up[:, :PAIRS], up[:, PAIRS:])
    parts = [v_a, u_a, pair(q, k, v, a_out), g_a, pair(g_b, b_out), w_o]
    for i in range(QUARTERS):
        parts.append(up[:, 2 * UPQ * i:2 * UPQ * (i + 1)])
        parts.append(flat(a["w_down"][:, i * UPQ * P:(i + 1) * UPQ * P]))
    stream = np.ascontiguousarray(np.concatenate(parts, axis=1)).reshape(L * UNITS, P, KT * P)

    vec = lambda x: x.reshape(L, -1, P)
    cols_h = np.concatenate([vec(a[n]) for n in ("b_ada", "g_pre_mix", "g_post_mix", "g_pre_ffn", "g_post_ffn",
                                                 "g_sgu", "conv_b", "conv_w")], axis=1)
    arrays = {
        "xT": a["x"][0].T.reshape(KT, P, S).transpose(1, 0, 2),
        "cvec": a["c"].reshape(1, D),
        "w_stream": stream,
        "w_ada_rows": a["w_ada"].transpose(0, 2, 1).reshape(L * MODS, P, D),
        "cols_d": cols_h.reshape(L * COLS, P).T,
        "w_sp": a["w_spatial"].transpose(0, 3, 1, 2).reshape(L, P, KT * P),
        "b_sp": a["b_spatial"].reshape(L, KT * P),
    }
    arrays = {k_: np.ascontiguousarray(v_) for k_, v_ in arrays.items()}
    nc = bacc.Bacc("TRN2", target_bir_lowering=False, num_devices=1, dynamic_dma_scratch_size=1024)
    args = [nc.dram_tensor(n, x.shape, mybir.dt.from_np(x.dtype), kind="ExternalInput").ap()
            for n, x in arrays.items()]
    out = nc.dram_tensor("outT", (P, KT, S), F32, kind="ExternalOutput").ap()
    build(nc, *args, out)
    r = run(nc, [arrays], core_ids=[0])
    y = r.results[0]["outT"]
    return y.transpose(1, 0, 2).reshape(D, S).T.reshape(1, S, D)
```

```python
from contextlib import ExitStack

import concourse.bass as bass
from concourse import mybir

F32 = mybir.dt.float32
F32R = mybir.dt.float32r
BF16 = mybir.dt.bfloat16
ALU = mybir.AluOpType
ACT = mybir.ActivationFunctionType

P = 128
D = 1024
S = 512
DEPTH = 2
KT = D // P
NC = S // P
HEADS = 8
DFF = 4 * D
QUARTERS = 4
PAIRS = DFF // P
SCALE = float(P) ** -0.5
EPS = 1e-6
HALF = S // 2

U_V = 0
U_U = U_V + KT
U_HEAD = U_U + KT
U_GA = U_HEAD + 4 * HEADS
U_GB = U_GA + KT
U_O = U_GB + 2 * KT
U_FFN = U_O + KT
UPQ = PAIRS // QUARTERS
FQ = 2 * UPQ + KT
UNITS = U_FFN + QUARTERS * FQ
RING = 4
RAW = 2

POSTED = {8: (0, 1, 2), 9: (3, 4, 5), 10: (6, 7)}
DN_ITEMS = (QUARTERS - 1) * KT + 12


def wo_item(k):
    if k < 4:
        return k, slice(0, S)
    return 4 + k % 4, half(0 if k < 8 else 1)


C_BADA = 0
C_GPREM = 48
C_GPOSTM = 56
C_GPREF = 64
C_GPOSTF = 72
C_GSGU = 80
C_CB = 88
C_CW = C_CB + 2 * PAIRS
COLS = C_CW + 3 * 2 * PAIRS
SHIFT_M, SCALE_M, GATE_M, SHIFT_F, SCALE_F, GATE_F = (8 * i for i in range(6))
MODS = 48
ADA_FIRST = 16
ADA_IN = MODS - ADA_FIRST
ADA_USES = ADA_IN + 1 + ADA_FIRST


def half(hf):
    return slice(hf * HALF, (hf + 1) * HALF)


def n_keys(j):
    return S - P * j


def build(nc, xT, cvec, w_stream, w_ada, cols_d, w_sp, b_sp, outT):
    with ExitStack() as ctx:
        def sb(name, shape, dt=F32):
            return ctx.enter_context(nc.sbuf_tensor(name, shape, dt))

        def sem(name):
            return ctx.enter_context(nc.semaphore(name))

        X = sb("X", [P, KT, S])
        HH, HL = sb("HH", [P, KT, S], F32R), sb("HL", [P, KT, S], F32R)
        AH, AL = sb("AH", [P, KT, S], F32R), sb("AL", [P, KT, S], F32R)
        OH, OL = sb("OH", [P, KT, S], F32R), sb("OL", [P, KT, S], F32R)
        M = sb("M", [P, KT, S])
        raw = sb("raw", [P, RAW, D])
        WH, WL = sb("WH", [P, RING, KT, P], F32R), sb("WL", [P, RING, KT, P], F32R)
        SC = sb("SC", [P, 14 * S], F32R)
        T = sb("T", [P, 5, S])
        ada = sb("ada", [P, D])
        cact = sb("cact", [P, D])
        cols = sb("cols", [P, DEPTH * COLS])
        mod = sb("mod", [P, DEPTH * MODS])
        acc = sb("acc", [P, ADA_FIRST])
        coef = sb("coef", [P, 3, KT])
        eps = sb("eps", [P, 1])
        ident = sb("ident", [P, P])
        ones = sb("ones", [P, P])
        diag = sb("diag", [P, 2, P])
        roots = sb("roots", [P, 2, 2])
        ntri, nones = sb("ntri", [P, P], F32R), sb("nones", [P, P], F32R)
        strict, negm = sb("strict", [P, P], BF16), sb("negm", [P, P], BF16)
        stats = sb("stats", [P, NC, 2, 6])
        mv = sb("mv", [P, NC, 2])
        rstd = sb("rstd", [P, NC])

        off = {j: sum(n_keys(i) for i in range(j)) for j in range(NC)}
        SPH = {j: SC[:, off[j]:off[j] + n_keys(j)] for j in range(NC)}
        SPL = {j: SC[:, 1280 + off[j]:1280 + off[j] + n_keys(j)] for j in range(NC)}
        ATH = {j: SPH[0] if j == 0 else SC[:, 2560 + off[j] - S:2560 + off[j] - S + n_keys(j)] for j in range(NC)}
        ATL = {j: SPL[0] if j == 0 else SC[:, 3328 + off[j] - S:3328 + off[j] - S + n_keys(j)] for j in range(NC)}
        QH, QL, KH, KL, VH, VL = (SC[:, 4096 + S * i:4096 + S * (i + 1)] for i in range(6))
        WSH, WSL = SC[:, 0:D], SC[:, D:2 * D]
        M_tok = M[:, :, :].rearrange("p m t -> p (m t)").rearrange("p (c d) -> p c d", c=NC)
        ADA0 = [T[:, 0:2].rearrange("p a b -> p (a b)"), T[:, 3:5].rearrange("p a b -> p (a b)"), ada[:, :]]
        Y_BANKS, X_BANKS = (6, 5), (7, 6)
        GA_BANKS = (0, 1, 2, 4)
        GB_BANKS = (5, 6, 7, 3)

        ps = [ctx.enter_context(nc.psum_tensor(f"ps{i}", [P, S], F32)) for i in range(8)]

        w_landed = [sem(f"w_landed{i}") for i in range(RAW)]
        w_hi, w_split, unit_done = sem("w_hi"), sem("w_split"), sem("unit_done")
        half_done = sem("half_done")
        x_landed, cols_landed, c_landed = sem("x_landed"), sem("cols_landed"), sem("c_landed")
        ada_landed, ada_used, ada_first = sem("ada_landed"), sem("ada_used"), sem("ada_first")
        ada0_landed = [sem(f"ada0_landed{i}") for i in range(3)]
        c_ready = sem("c_ready")
        bsp_landed, ws_landed = sem("bsp_landed"), sem("ws_landed")
        pool_consts, dve_consts = sem("pool_consts"), sem("dve_consts")
        ws_split = sem("ws_split")
        xsq, xsum, xroot, x_inv, x_bc = (sem(n) for n in ("xsq", "xsum", "xroot", "x_inv", "x_bc"))
        xsq_added, xnorm, h_hi, h_ready = sem("xsq_added"), sem("xnorm"), sem("h_hi"), sem("h_ready")
        y_sq, y_acc, y_sum, y_tail = (sem(n) for n in ("y_sq", "y_acc", "y_sum", "y_tail"))
        y_root, y_inv, y_bc, x_new = (sem(n) for n in ("y_root", "y_inv", "y_bc", "x_new"))
        v_gelu, v_tr, v_copied = sem("v_gelu"), sem("v_tr"), sem("v_copied")
        ln_var, ln_root, vn_ready = sem("ln_var"), sem("ln_root"), sem("vn_ready")
        u_gelu, f_done, a_ready = sem("u_gelu"), sem("f_done"), sem("a_ready")
        q_evac, k_evac, vb_evac, ao_evac = sem("q_evac"), sem("k_evac"), sem("vb_evac"), sem("ao_evac")
        q_split, k_split, vb_tr, vb_split = sem("q_split"), sem("k_split"), sem("vb_tr"), sem("vb_split")
        z_done, ln1p, sp_ready, sfx = sem("z_done"), sem("ln1p"), sem("sp_ready"), sem("sfx")
        arg_masked, attn32, attn_ready = sem("arg_masked"), sem("attn32"), sem("attn_ready")
        av_done, o_split = sem("av_done"), sem("o_split")
        ga_sig, ga_used = sem("ga_sig"), sem("ga_used")
        gb_sig, merged = sem("gb_sig"), sem("merged")
        wo_evac = sem("wo_evac")
        tap2, conved, gelued, g_ready = sem("tap2"), sem("conved"), sem("gelued"), sem("g_ready")
        dn_added = sem("dn_added")
        out_landed = sem("out_landed")
        act_stage, dve_stage, pe_stage = sem("act_stage"), sem("dve_stage"), sem("pe_stage")

        block = ctx.enter_context(nc.Block())

        def next_layer(l, size, k):
            return nc.s_assert_within(l * size + k + size, size, DEPTH * size - 1,
                                      skip_runtime_bounds_check_because="only where l + 1 is a layer")

        def col(l, c):
            return cols[:, bass.ds(l * COLS + c, 1)]

        @block.sync
        def _(sp):
            for k in range(ADA_FIRST):
                if k >= 3:
                    sp.wait_ge(ada_first, k - 2)
                sp.dma_start(ADA0[k % 3], w_ada[k // 2 + (SCALE_M if k % 2 else SHIFT_M)]
                             ).then_inc(ada0_landed[k % 3], 16)
                if k == 2:
                    sp.dma_start(X[:, :, :], xT).then_inc(x_landed, 16)
                if k == 5:
                    for n in range(RAW):
                        sp.dma_start(raw[:, n], w_stream[n]).then_inc(w_landed[n], 16)
                if k == 9:
                    for n in range(RAW, RING):
                        sp.wait_ge(w_split, n - RAW + 1)
                        sp.dma_start(raw[:, n % RAW], w_stream[n]).then_inc(w_landed[n % RAW], 16)
            with sp.Fori(1, DEPTH * UNITS // RAW - 1) as i:
                for s in range(RAW):
                    sp.wait_ge(w_split, i * RAW + (s + 1))
                    sp.dma_start(raw[:, s], w_stream[bass.ds(i * RAW + (s + RAW), 1)].rearrange("o p n -> (o p) n")
                                 ).then_inc(w_landed[s], 16)
            final = DEPTH * 2 * 2 * KT
            sp.wait_ge(x_new, final + KT)
            sp.dma_start(outT[:, :, half(0)], X[:, :, half(0)]).then_inc(out_landed, 16)
            for m in range(0, KT, 2):
                sp.wait_ge(x_new, final + KT + (m + 2))
                sp.dma_start(outT[:, m:m + 2, half(1)], X[:, m:m + 2, half(1)]).then_inc(out_landed, 16)
            sp.wait_ge(out_landed, (1 + KT // 2) * 16)

        @block.gpsimd
        def _(pool):
            nc.gpsimd.memset(ones[:, :], 1.0).then_inc(pool_consts, 1)
            pool.wait_ge(pool_consts, 1)
            nc.gpsimd.affine_select(out=ident[:, :], in_=ones[:, :], pattern=[[-1, P]], compare_op=ALU.is_equal,
                                    fill=0.0, base=0, channel_multiplier=1)
            nc.gpsimd.affine_select(out=diag[:, 0], in_=ones[:, :], pattern=[[-1, P]], compare_op=ALU.is_ge,
                                    fill=0.0, base=0, channel_multiplier=1).then_inc(pool_consts, 1)

            def split(l, i):
                for s in range(RING):
                    pool.wait_ge(w_hi, l * UNITS + i * RING + (s + 1))
                    nc.gpsimd.tensor_tensor(WL[:, s].rearrange("p k n -> p (k n)"), raw[:, s % RAW],
                                            WH[:, s].rearrange("p k n -> p (k n)").bitcast(F32),
                                            ALU.subtract).then_inc(w_split, 1)

            def add_squares(n):
                t = half(1)
                pool.wait_ge(xsq, (n * 2 + 1) * KT + 1)
                for m in range(1, KT):
                    pool.wait_ge(xsq, (n * 2 + 1) * KT + (m + 1))
                    last = nc.gpsimd.tensor_tensor(M[:, 0, t], M[:, 0, t], M[:, m, t], ALU.add)
                    if m < KT - 1:
                        pool.drain()
                last.then_inc(xsq_added, 1)

            with pool.Fori(0, DEPTH) as l:
                split(l, 0)
                with pool.If(l > 0):
                    add_squares(2 * l)
                with pool.Fori(1, U_FFN // RING + 1) as i:
                    split(l, i)
                add_squares(2 * l + 1)
                with pool.Fori(U_FFN // RING + 1, UNITS // RING) as i:
                    split(l, i)

        @block.scalar
        def _(act):
            def split(l, i, n):
                act.wait_ge(w_landed[n % RAW], (l * (UNITS // RAW) + i * (RING // RAW) + (n // RAW + 1)) * 16)
                act.wait_ge(unit_done, l * UNITS + i * RING + (n + 1))
                nc.scalar.activation(WH[:, n % RING].rearrange("p k n -> p (k n)"), raw[:, n % RAW],
                                     ACT.Copy).then_inc(w_hi, 1)

            def ahead(l, i, base, s):
                split(l, i, base + s + RING)

            def ready(l, i, base, s):
                act.wait_ge(unit_done, l * UNITS + i * 4 + (base + s + 1 + RING))

            def load_ada(l, j):
                act.wait_ge(ada_used, l * ADA_USES + j + 2)
                act.dma_start(ada[:, :], w_ada[bass.ds(l * MODS + (j + ADA_FIRST), 1)].rearrange("o p n -> (o p) n")
                              ).then_inc(ada_landed, 16)

            def square(n, hf, ms):
                for m in ms:
                    act.wait_ge(x_new, (n * 2 + hf) * KT + (m + 1))
                    nc.scalar.activation(M[:, m, half(hf)], X[:, m, half(hf)], ACT.Square).then_inc(xsq, 1)

            def root(bank, hf, which, rooted):
                nc.scalar.activation(roots[:, which], ps[bank][:, hf * HALF:hf * HALF + 2], ACT.Sqrt,
                                     bias=eps[:, 0:1], scale=1.0 / D).then_inc(rooted, 1)

            def t_added(n, k):
                if k < 10:
                    act.wait_ge(y_acc, n * 8 + (k + 1))
                else:
                    act.wait_ge(y_tail, n * 4 + (k - 9))

            def x_root(n, hf):
                act.wait_ge(xsum, n * 2 + (hf + 1))
                root(X_BANKS[hf], hf, 0, xroot)

            def y_root_of(n, hf):
                if hf == 0:
                    act.wait_ge(y_sum, n + 1)
                else:
                    act.wait_ge(y_tail, n * 4 + 4)
                root(Y_BANKS[hf], hf, 1, y_root)

            def shifted(n, hf, between=None):
                for m in range(KT):
                    if m == 2 and between:
                        between()
                    act.wait_ge(xnorm, (n * 2 + hf) * KT + (m + 1))
                    nc.scalar.activation(HH[:, m, half(hf)], M[:, m, half(hf)], ACT.Identity,
                                         bias=coef[:, 2, m:m + 1]).then_inc(h_hi, 1)

            act.sem_inc(wo_evac, 2)
            act.dma_start(cact[:, :], cvec.to_broadcast([P, D])).then_inc(c_landed, 16)
            act.dma_start(cols[:, :], cols_d).then_inc(cols_landed, 16)
            act.wait_ge(c_landed, 16)
            nc.scalar.activation(cact[:, :], cact[:, :], ACT.Silu).then_inc(c_ready, 1)
            act.wait_ge(x_landed, 16)
            act.wait_ge(dve_consts, 1)
            square(0, 0, range(KT))
            square(0, 1, range(KT))
            for n in range(RAW):
                split(0, 0, n)
            x_root(0, 0)
            act.wait_ge(x_inv, 1)
            x_root(0, 1)
            for n in range(RAW, RING):
                split(0, 0, n)
            shifted(0, 0)
            act.sem_inc(act_stage, 1)
            with act.Fori(0, DEPTH) as l:
                with act.If(l > 0):
                    square(2 * l, 1, range(KT))
                    x_root(2 * l, 1)
                shifted(2 * l, 1)
                act.wait_ge(ada_used, l * ADA_USES + 1)
                act.dma_start(ada[:, :], w_sp[bass.ds(l, 1)].rearrange("o p n -> (o p) n")).then_inc(ws_landed, 16)

                nc.scalar.preload_act_table(ACT.Gelu)
                with act.Fori(0, KT // 4) as i:
                    for s in range(4):
                        ready(l, i, U_V, s)
                        act.wait_ge(v_tr, l * KT + i * 4 + (s + 1))
                        nc.scalar.activation(T[:, s], ps[s][:, :], ACT.Gelu).then_inc(v_gelu, 1)
                        ahead(l, i, U_V, s)
                act.wait_ge(ws_split, l + 1)
                act.dma_start(ada[:, :], b_sp[bass.ds(l, 1)].to_broadcast([P, D])).then_inc(bsp_landed, 16)
                act.wait_ge(ln_var, l + 1)
                nc.scalar.activation(rstd[:, :], mv[:, :, 1], ACT.Sqrt, bias=eps[:, 0:1]).then_inc(ln_root, 1)
                with act.Fori(0, KT // 4) as i:
                    for s in range(4):
                        ready(l, i, U_U, s)
                        act.wait_ge(v_tr, l * KT + (s + 1 + KT))
                        act.wait_ge(a_ready, l * KT + i * 4 + (s + 1))
                        nc.scalar.activation(T[:, s], ps[s][:, :], ACT.Gelu).then_inc(u_gelu, 1)
                        ahead(l, i, U_U, s)

                nc.scalar.preload_act_table_set("natural_log_exp_and_others")

                def exps(h, js):
                    for j in js:
                        act.wait_ge(arg_masked, l * 32 + h * 4 + (NC - j))
                        if j < 2:
                            act.wait_ge(attn_ready, l * 32 + h * 4 + (NC - j - 2))
                        nc.scalar.activation(T[:, 3 + j % 2, 0:n_keys(j)], ps[4 + j][:, 0:n_keys(j)],
                                             ACT.Exp).then_inc(attn32, 1)

                def head(h, first):
                    base = U_HEAD
                    ready(l, h, base, 0)
                    act.wait_ge(q_split, l * HEADS + h + 1)
                    nc.scalar.activation(T[:, 0], ps[0][:, :], ACT.Copy, scale=SCALE).then_inc(q_evac, 1)
                    ahead(l, h, base, 0)
                    load_ada(l, h * 2)
                    if not first:
                        exps(h - 1, (3, 2))
                    ready(l, h, base, 1)
                    act.wait_ge(k_split, l * HEADS + h + 1)
                    nc.scalar.activation(T[:, 1], ps[1][:, :], ACT.Copy).then_inc(k_evac, 1)
                    ahead(l, h, base, 1)
                    if not first:
                        exps(h - 1, (1, 0))
                    ready(l, h, base, 2)
                    act.wait_ge(vb_tr, l * HEADS + h + 1)
                    nc.scalar.activation(T[:, 2], ps[0][:, :], ACT.Copy).then_inc(vb_evac, 1)
                    ahead(l, h, base, 2)
                    load_ada(l, h * 2 + 1)
                    for j in (3, 2, 1, 0):
                        n = n_keys(j)
                        e = T[:, 3 + j % 2, 0:n]
                        act.wait_ge(z_done, l * 32 + h * 4 + (NC - j))
                        if j < 2:
                            act.wait_ge(sp_ready, l * 32 + h * 4 + (NC - j - 2))
                        elif not first:
                            act.wait_ge(attn_ready, l * 32 + h * 4)
                        nc.scalar.activation(e, ps[4 + j][:, 0:n], ACT.Abs)
                        act.drain()
                        nc.scalar.activation(e, e, ACT.Exp, scale=-1.0)
                        act.drain()
                        nc.scalar.activation(e, e, ACT.Ln, bias=1.0).then_inc(ln1p, 1)
                    ready(l, h, base, 3)
                    nc.scalar.activation(M[:, bass.ds(h, 1)].rearrange("p o t -> p (o t)"), ps[1][:, :],
                                         ACT.Copy).then_inc(ao_evac, 1)
                    ahead(l, h, base, 3)

                act.wait_ge(a_ready, l * KT + (KT + 2))
                head(0, True)
                with act.Fori(1, HEADS) as h:
                    head(h, False)
                for u in range(KT):
                    ready(l, u // 4, U_GA, u % 4)
                    if u == 0:
                        exps(HEADS - 1, (3, 2))
                    if u == 1:
                        exps(HEADS - 1, (1, 0))
                    if u >= 2:
                        for v in (0, 1, 2) if u == 2 else (u,):
                            if v >= 4:
                                act.wait_ge(ga_used, l * KT + v - 4 + 1 + 4)
                            if v == 3:
                                act.wait_ge(attn_ready, l * 32 + 32)
                            nc.scalar.activation(T[:, v % 4], ps[GA_BANKS[v % 4]][:, :], ACT.Sigmoid
                                                 ).then_inc(ga_sig, 1)
                    ahead(l, u // 4, U_GA, u % 4)
                act.wait_ge(ga_used, l * KT + (KT + 4))
                act.sem_inc(act_stage, 1)
                with act.Fori(0, KT // 2) as i:
                    for s in range(4):
                        if s % 2 == 0:
                            ready(l, i, U_GB, s)
                            act.wait_ge(merged, l * KT + i * 2 + (s // 2 + 1))
                            nc.scalar.activation(T[:, s], ps[GB_BANKS[s]][:, :], ACT.Sigmoid).then_inc(gb_sig, 1)
                        ahead(l, i, U_GB, s)
                        load_ada(l, i * 4 + (2 * HEADS + s))
                nc.scalar.preload_act_table(ACT.Sqrt)
                act.wait_ge(merged, l * KT + (KT + 2))

                def wo_out(k):
                    u, cols_ = wo_item(k)
                    if 4 <= k < 8:
                        act.wait_ge(half_done, l * 8 + (k - 4 + 1))
                    else:
                        ready(l, u // 4, U_O, u % 4)
                    t_added(2 * l, k)
                    nc.scalar.activation(T[:, k % 2, cols_], ps[k % 2][:, cols_], ACT.Square).then_inc(y_sq, 1)
                    nc.scalar.activation(M[:, u, cols_], ps[k % 2][:, cols_], ACT.Copy).then_inc(wo_evac, 1)

                for k in range(8):
                    wo_out(k)
                    if k < 4:
                        ahead(l, 0, U_O, k)
                y_root_of(2 * l, 0)
                for k in (8, 9):
                    wo_out(k)
                    ahead(l, 1, U_O, k - 8)
                    square(2 * l + 1, 0, POSTED[k])
                wo_out(10)
                square(2 * l + 1, 0, POSTED[10])
                ahead(l, 1, U_O, 2)
                wo_out(11)
                x_root(2 * l + 1, 0)
                y_root_of(2 * l, 1)
                shifted(2 * l + 1, 0, lambda: ahead(l, 1, U_O, 3))
                square(2 * l + 1, 1, range(KT))
                x_root(2 * l + 1, 1)
                shifted(2 * l + 1, 1)

                def tap(l, q, i, s):
                    tile = q * UPQ + i * 2 + (s // 2 + PAIRS * (s % 2))
                    act.wait_ge(g_ready, (l * QUARTERS + q) * UPQ + i * 2 + (s // 2 + 1))
                    nc.scalar.activation(T[:, s], ps[s][:, :], ACT.Identity, scale=col(l, tile + (C_CW + 4 * PAIRS)),
                                         bias=col(l, tile + C_CB)).then_inc(tap2, 1)

                def quarter(q, last):
                    with act.Fori(0, UPQ // 2) as i:
                        for s in range(4):
                            n = q * (FQ // 4) + i
                            ready(l, n, U_FFN, s)
                            tap(l, q, i, s)
                            ahead(l, n, U_FFN, s)
                            if s == 0:
                                with act.If(l < DEPTH - 1):
                                    k = q * (UPQ // 2) + i
                                    act.wait_ge(ada_used, l * ADA_USES + k + (ADA_IN + 2))
                                    act.dma_start(ada[:, :], w_ada[bass.ds(next_layer(l, MODS, k), 1)].rearrange(
                                        "o p n -> (o p) n")).then_inc(ada_landed, 16)
                            if s % 2:
                                act.wait_ge(conved, ((l * QUARTERS + q) * UPQ + i * 2) * 2 + (s + 4))
                                nc.scalar.activation(T[:, s - 1], T[:, s - 1], ACT.Gelu_apprx_tanh
                                                     ).then_inc(gelued, 1)
                    if not last:
                        for i in range(KT // 4):
                            for s in range(4):
                                ahead(l, q * (FQ // 4) + (2 * UPQ // 4 + i), U_FFN, s)

                def dn_square(k):
                    u, cols_ = wo_item(k)
                    act.wait_ge(dn_added, l * DN_ITEMS + (DN_ITEMS - 12 + k + 1 + 2))
                    t_added(2 * l + 1, k)
                    nc.scalar.activation(T[:, k % 2, cols_], M[:, u, cols_], ACT.Square).then_inc(y_sq, 1)

                act.wait_ge(g_ready, l * PAIRS + 2)
                act.sem_inc(act_stage, 1)
                with act.Fori(0, QUARTERS - 1) as q:
                    quarter(q, False)
                act.wait_ge(g_ready, (l + 1) * PAIRS + 2 - UPQ)
                quarter(QUARTERS - 1, True)
                nc.scalar.preload_act_table(ACT.Sqrt)
                for k in range(8):
                    dn_square(k)
                    if k < 4:
                        ahead(l, (QUARTERS - 1) * (FQ // 4) + 2 * UPQ // 4, U_FFN, k)
                y_root_of(2 * l + 1, 0)
                with act.If(l < DEPTH - 1):
                    for k in (8, 9):
                        dn_square(k)
                        split(l + 1, 0, k - 8)
                        square(2 * l + 2, 0, POSTED[k])
                    dn_square(10)
                    square(2 * l + 2, 0, POSTED[10])
                    split(l + 1, 0, 2)
                    dn_square(11)
                    x_root(2 * l + 2, 0)
                    y_root_of(2 * l + 1, 1)
                    shifted(2 * l + 2, 0, lambda: split(l + 1, 0, 3))
                with act.Else():
                    for k in range(8, 12):
                        dn_square(k)
                    y_root_of(2 * l + 1, 1)

        @block.vector
        def _(dve):
            def ready(l, i, base, s):
                dve.wait_ge(unit_done, l * UNITS + i * 4 + (base + s + 1 + RING))

            def hi_lo(hi, lo, src, done):
                nc.vector.tensor_copy(hi, src)
                dve.drain()
                return nc.vector.tensor_tensor(lo, src, hi.bitcast(F32), ALU.subtract).then_inc(done, 1)

            def ada_unit(l, j):
                dve.wait_ge(ada_landed, l * MODS * 16 + (j + 1) * 16)
                nc.vector.tensor_tensor_reduce(out=ada[:, :], in0=ada[:, :], in1=cact[:, :], scale=1.0, scalar=0.0,
                                               op0=ALU.mult, op1=ALU.add, accum_out=acc[:, 0:1]).then_inc(ada_used, 1)
                dve.drain()
                nc.vector.tensor_tensor(mod[:, bass.ds(l * MODS + j + ADA_FIRST, 1)], acc[:, 0:1],
                                        col(l, j + (C_BADA + ADA_FIRST)), ALU.add)
                dve.drain()

            def modulation(sh, sc, g):
                nc.vector.tensor_copy(coef[:, 2], mod[:, bass.ds(sh, KT)])
                nc.vector.scalar_tensor_tensor(out=coef[:, 0], in0=mod[:, bass.ds(sc, KT)], scalar=1.0,
                                               in1=cols[:, bass.ds(g, KT)], op0=ALU.add, op1=ALU.mult)
                dve.drain()

            def inverse(which, rooted, inverted, count):
                dve.wait_ge(rooted, count)
                nc.vector.reciprocal(roots[:, which], roots[:, which])
                dve.drain()
                for c in range(2):
                    ins = nc.vector.tensor_scalar(diag[:, c], ident[:, :], roots[:, which, c:c + 1], None, ALU.mult)
                ins.then_inc(inverted, 1)

            def x_inverse(n, hf):
                inverse(0, xroot, x_inv, n * 2 + (hf + 1))

            def y_inverse(n, hf):
                inverse(1, y_root, y_inv, n * 2 + (hf + 1))

            def normed(n, hf, m):
                nc.vector.scalar_tensor_tensor(out=M[:, m, half(hf)], in0=X[:, m, half(hf)],
                                               scalar=coef[:, 0, m:m + 1], in1=ps[X_BANKS[hf]][:, half(hf)],
                                               op0=ALU.mult, op1=ALU.mult).then_inc(xnorm, 1)

            def norm_low(n, hf, m):
                dve.wait_ge(h_hi, (n * 2 + hf) * KT + (m + 1))
                nc.vector.scalar_tensor_tensor(out=HL[:, m, half(hf)], in0=M[:, m, half(hf)],
                                               scalar=coef[:, 2, m:m + 1], in1=HH[:, m, half(hf)].bitcast(F32),
                                               op0=ALU.add, op1=ALU.subtract).then_inc(h_ready, 1)

            def norm(n, hf, between={}):
                dve.wait_ge(x_bc, n * 2 + (hf + 1))
                for m in range(KT):
                    if m in between:
                        between[m]()
                    normed(n, hf, m)
                    if m:
                        norm_low(n, hf, m - 1)
                norm_low(n, hf, KT - 1)
                dve.drain()

            def post_coef(l, which):
                gate, g = (GATE_F, C_GPOSTF) if which else (GATE_M, C_GPOSTM)
                nc.vector.scalar_tensor_tensor(out=coef[:, 1], in0=mod[:, bass.ds(l * MODS + gate, KT)], scalar=1.0,
                                               in1=cols[:, bass.ds(l * COLS + g, KT)], op0=ALU.add, op1=ALU.mult)
                dve.drain()

            def add_squares(n, k):
                _, cols_ = wo_item(k)
                dve.wait_ge(y_sq, n * 12 + (k + 1))
                nc.vector.tensor_tensor(T[:, 2, cols_], T[:, 2, cols_], T[:, k % 2, cols_], ALU.add
                                        ).then_inc(y_acc, 1)
                dve.drain()

            def post(n, hf, ms):
                t = half(hf)
                dve.wait_ge(y_bc, n * 2 + (hf + 1))
                for m in ms:
                    nc.vector.scalar_tensor_tensor(out=M[:, m, t], in0=M[:, m, t], scalar=coef[:, 1, m:m + 1],
                                                   in1=ps[Y_BANKS[hf]][:, t], op0=ALU.mult, op1=ALU.mult)
                dve.drain()
                for m in ms:
                    nc.vector.tensor_tensor(X[:, m, t], X[:, m, t], M[:, m, t], ALU.add).then_inc(x_new, 1)

            dve.sem_inc(ada_used, 1)
            dve.sem_inc(v_copied, 2)
            dve.sem_inc(a_ready, 4)
            dve.sem_inc(q_split, 1)
            dve.sem_inc(k_split, 1)
            dve.sem_inc(o_split, 1)
            dve.sem_inc(vb_split, 1)
            dve.sem_inc(ga_used, 4)
            dve.sem_inc(merged, 2)
            dve.sem_inc(conved, 4)
            dve.sem_inc(g_ready, 2)
            dve.sem_inc(dn_added, 2)
            dve.sem_inc(y_acc, 2)
            dve.sem_inc(x_new, 2 * KT)
            dve.wait_ge(pool_consts, 2)
            nc.vector.memset(eps[:, :], EPS)
            nc.vector.tensor_scalar(ntri[:, :], diag[:, 0], -1.0, None, ALU.mult)
            nc.vector.tensor_scalar(nones[:, :], ones[:, :], -1.0, None, ALU.mult)
            nc.vector.tensor_scalar(strict[:, :], diag[:, 0], -1.0, 1.0, ALU.mult, ALU.add)
            nc.vector.tensor_scalar(negm[:, :], diag[:, 0], -1e30, None, ALU.mult).then_inc(dve_consts, 1)
            dve.drain()
            dve.wait_ge(c_ready, 1)
            tiles = {9: (0, 1, 2), 11: (3, 4), 13: (5, 6), 15: (7,)}
            for k in range(ADA_FIRST):
                dve.wait_ge(ada0_landed[k % 3], 16 * (k // 3 + 1))
                row = k // 2 + (SCALE_M if k % 2 else SHIFT_M)
                nc.vector.tensor_tensor_reduce(out=ADA0[k % 3], in0=ADA0[k % 3], in1=cact[:, :], scale=1.0,
                                               scalar=0.0, op0=ALU.mult, op1=ALU.add,
                                               accum_out=acc[:, row:row + 1]).then_inc(ada_first, 1)
                if k == 7:
                    x_inverse(0, 0)
                if k == 9:
                    dve.wait_ge(cols_landed, 16)
                if k in tiles:
                    m0, m1 = tiles[k][0], tiles[k][-1] + 1
                    dve.drain()
                    for j in (SHIFT_M, SCALE_M):
                        nc.vector.tensor_tensor(mod[:, j + m0:j + m1], acc[:, j + m0:j + m1],
                                                cols[:, C_BADA + j + m0:C_BADA + j + m1], ALU.add)
                    dve.drain()
                    nc.vector.tensor_copy(coef[:, 2, m0:m1], mod[:, SHIFT_M + m0:SHIFT_M + m1])
                    nc.vector.scalar_tensor_tensor(out=coef[:, 0, m0:m1], in0=mod[:, SCALE_M + m0:SCALE_M + m1],
                                                   scalar=1.0, in1=cols[:, C_GPREM + m0:C_GPREM + m1],
                                                   op0=ALU.add, op1=ALU.mult)
                    dve.drain()
                    if k == 9:
                        dve.wait_ge(x_landed, 16)
                        dve.wait_ge(x_bc, 1)
                        x_inverse(0, 1)
                    for m in tiles[k]:
                        normed(0, 0, m)
                        if m:
                            norm_low(0, 0, m - 1)
            norm_low(0, 0, KT - 1)
            dve.drain()

            with dve.Fori(0, DEPTH) as l:
                with dve.If(l > 0):
                    for m in range(0, KT, 2):
                        post(2 * l - 1, 1, (m, m + 1))
                    x_inverse(2 * l, 1)
                norm(2 * l, 1)
                for g in range(KT):
                    if g == 4:
                        dve.wait_ge(ws_landed, l * 16 + 16)
                        nc.vector.tensor_tensor(diag[:, 0], strict[:, :], ident[:, :], ALU.add)
                        dve.drain()
                        ws = ada[:, :].rearrange("p (g t) -> p g t", g=KT)
                        nc.vector.tensor_tensor(ws, ws, diag[:, 0].unsqueeze(1).to_broadcast([P, KT, P]), ALU.mult)
                        dve.drain()
                        hi_lo(WSH, WSL, ada[:, :], ws_split)
                    dve.wait_ge(v_tr, l * KT + (g + 1 + 4))
                    nc.vector.tensor_copy(M_tok[:, :, g * P:(g + 1) * P],
                                          ps[4 + g % 2][:, :].rearrange("p (c d) -> p c d", c=NC)
                                          ).then_inc(v_copied, 1)
                dve.drain()
                for c in range(NC):
                    for part in range(2):
                        nc.vector.bn_stats(stats[:, c, part], M_tok[:, c, part * S:(part + 1) * S])
                dve.drain()
                for c in range(NC):
                    ins = nc.vector.bn_aggr(mv[:, c], stats[:, c])
                ins.then_inc(ln_var, 1)
                dve.wait_ge(ln_root, l + 1)
                nc.vector.reciprocal(rstd[:, :], rstd[:, :])
                dve.drain()
                for c in range(NC):
                    nc.vector.tensor_scalar(M_tok[:, c], M_tok[:, c], mv[:, c, 0:1], rstd[:, c:c + 1], ALU.subtract,
                                            ALU.mult)
                dve.drain()
                for c in range(NC):
                    src = M_tok[:, c].rearrange("p (g d) -> p g d", g=KT)
                    nc.vector.tensor_copy(AH[:, :, c * P:(c + 1) * P], src)
                dve.drain()
                for c in range(NC):
                    src = M_tok[:, c].rearrange("p (g d) -> p g d", g=KT)
                    nc.vector.tensor_tensor(AL[:, :, c * P:(c + 1) * P], src,
                                            AH[:, :, c * P:(c + 1) * P].bitcast(F32),
                                            ALU.subtract).then_inc(vn_ready, 1)

                dve.wait_ge(bsp_landed, l * 16 + 16)
                dve.sem_inc(dve_stage, 1)
                with dve.Fori(0, KT // 4) as i:
                    for s in range(4):
                        g = i * 4 + s
                        dve.wait_ge(f_done, l * KT + g + 1)
                        dve.wait_ge(u_gelu, l * KT + g + 1)
                        f = ps[4 + s % 2][:, :]
                        bias = ada[:, bass.ds(g * P, P)].unsqueeze(1).to_broadcast([P, NC, P])
                        fc = f.rearrange("p (c t) -> p c t", c=NC)
                        nc.vector.scalar_tensor_tensor(out=fc, in0=fc, scalar=col(l, g + C_GSGU), in1=bias,
                                                       op0=ALU.mult, op1=ALU.add)
                        dve.drain()
                        nc.vector.tensor_tensor(T[:, s], T[:, s], f, ALU.mult)
                        dve.drain()
                        hi_lo(AH[:, bass.ds(g, 1)].rearrange("p o t -> p (o t)"),
                              AL[:, bass.ds(g, 1)].rearrange("p o t -> p (o t)"), T[:, s], a_ready)
                dve.drain().then_inc(ada_used, 1)

                def attn(h, js):
                    for j in js:
                        n = n_keys(j)
                        dve.wait_ge(sfx, l * 32 + h * 4 + (NC - j))
                        nc.vector.tensor_tensor(ps[4 + j][:, 0:P], ps[4 + j][:, 0:P], negm[:, :],
                                                ALU.add).then_inc(arg_masked, 1)
                        dve.wait_ge(attn32, l * 32 + h * 4 + (NC - j))
                        hi_lo(ATH[j], ATL[j], T[:, 3 + j % 2, 0:n], attn_ready)

                def out_split(h):
                    dve.wait_ge(av_done, l * HEADS + h + 1)
                    hi_lo(OH[:, bass.ds(h, 1)].rearrange("p o t -> p (o t)"),
                          OL[:, bass.ds(h, 1)].rearrange("p o t -> p (o t)"), ps[3][:, :], o_split)

                def head(h, first):
                    dve.wait_ge(q_evac, l * HEADS + h + 1)
                    hi_lo(QH, QL, T[:, 0], q_split)
                    if not first:
                        attn(h - 1, (3, 2))
                    dve.wait_ge(k_evac, l * HEADS + h + 1)
                    hi_lo(KH, KL, T[:, 1], k_split)
                    if not first:
                        attn(h - 1, (1, 0))
                    ada_unit(l, h * 2)
                    if not first:
                        out_split(h - 1)
                    for j in (3, 2, 1, 0):
                        n = n_keys(j)
                        e = T[:, 3 + j % 2, 0:n]
                        dve.wait_ge(ln1p, l * 32 + h * 4 + (NC - j))
                        nc.vector.scalar_tensor_tensor(out=e, in0=ps[4 + j][:, 0:n], scalar=0.0, in1=e, op0=ALU.max,
                                                       op1=ALU.add)
                        dve.drain()
                        nc.vector.tensor_tensor(e[:, 0:P], e[:, 0:P], strict[:, :], ALU.mult)
                        dve.drain()
                        hi_lo(SPH[j], SPL[j], e, sp_ready)
                    dve.wait_ge(vb_tr, l * HEADS + h + 1 + 1)
                    hi_lo(VH, VL, ps[2][:, :], vb_split)
                    ada_unit(l, h * 2 + 1)

                head(0, True)
                with dve.Fori(1, HEADS) as h:
                    head(h, False)
                attn(HEADS - 1, (3, 2, 1, 0))
                out_split(HEADS - 1)

                dve.wait_ge(ao_evac, l * HEADS + HEADS)
                dve.sem_inc(dve_stage, 1)
                with dve.Fori(0, KT // 4) as i:
                    for s in range(4):
                        m = M[:, bass.ds(i * 4 + s, 1)].rearrange("p o t -> p (o t)")
                        dve.wait_ge(ga_sig, l * KT + i * 4 + (s + 1))
                        nc.vector.tensor_tensor(m, m, T[:, s], ALU.mult).then_inc(ga_used, 1)
                dve.drain()
                with dve.Fori(0, KT // 2) as i:
                    for s in (1, 3):
                        g = i * 2 + s // 2
                        dve.wait_ge(gb_sig, l * KT + g + 1)
                        ready(l, i, U_GB, s)
                        nc.vector.tensor_tensor(T[:, s - 1], T[:, s - 1], ps[GB_BANKS[s]][:, :], ALU.mult)
                        dve.drain()
                        nc.vector.tensor_tensor(T[:, s - 1], T[:, s - 1],
                                                M[:, bass.ds(g, 1)].rearrange("p o t -> p (o t)"), ALU.add)
                        dve.drain()
                        hi_lo(AH[:, bass.ds(g, 1)].rearrange("p o t -> p (o t)"),
                              AL[:, bass.ds(g, 1)].rearrange("p o t -> p (o t)"), T[:, s - 1], merged)
                        ada_unit(l, i * 4 + (2 * HEADS + s - 1))
                        ada_unit(l, i * 4 + (2 * HEADS + s))
                modulation(l * MODS + SHIFT_F, l * MODS + SCALE_F, l * COLS + C_GPREF)
                post_coef(l, 0)
                nc.vector.memset(T[:, 2], 0.0)
                dve.drain()
                for k in range(8):
                    add_squares(2 * l, k)
                y_inverse(2 * l, 0)
                dve.wait_ge(wo_evac, l * 12 + (8 + 2))
                for ms in POSTED.values():
                    post(2 * l, 0, ms)
                x_inverse(2 * l + 1, 0)
                norm(2 * l + 1, 0, {2: lambda: y_inverse(2 * l, 1)})
                dve.wait_ge(wo_evac, l * 12 + (12 + 2))
                for m in range(0, KT, 2):
                    post(2 * l, 1, (m, m + 1))
                x_inverse(2 * l + 1, 1)
                norm(2 * l + 1, 1)

                def quarter(q, last):
                    with dve.Fori(0, UPQ // 2) as i:
                        for s in range(4):
                            tile = q * UPQ + i * 2 + (s // 2 + PAIRS * (s % 2))
                            dve.wait_ge(tap2, ((l * QUARTERS + q) * UPQ + i * 2) * 2 + (s + 1))
                            nc.vector.scalar_tensor_tensor(out=T[:, s, 1:S], in0=ps[s][:, 0:S - 1],
                                                           scalar=col(l, tile + (C_CW + 2 * PAIRS)), in1=T[:, s, 1:S],
                                                           op0=ALU.mult, op1=ALU.add)
                            dve.drain()
                            nc.vector.scalar_tensor_tensor(out=T[:, s, 2:S], in0=ps[s][:, 0:S - 2],
                                                           scalar=col(l, tile + C_CW), in1=T[:, s, 2:S],
                                                           op0=ALU.mult, op1=ALU.add).then_inc(conved, 1)
                            if s % 2:
                                g = i * 2 + s // 2
                                dve.drain()
                                dve.wait_ge(gelued, (l * QUARTERS + q) * UPQ + g + 1)
                                nc.vector.tensor_tensor(T[:, s], T[:, s - 1], T[:, s], ALU.mult)
                                dve.drain()
                                hi_lo(OH[:, bass.ds(g, 1)].rearrange("p o t -> p (o t)"),
                                      OL[:, bass.ds(g, 1)].rearrange("p o t -> p (o t)"), T[:, s], g_ready)
                            if s == 3:
                                with dve.If(l < DEPTH - 1):
                                    k = q * (UPQ // 2) + i
                                    dve.wait_ge(ada_landed, (l * MODS + k + (ADA_IN + 1)) * 16)
                                    nc.vector.tensor_tensor_reduce(
                                        out=ada[:, :], in0=ada[:, :], in1=cact[:, :], scale=1.0, scalar=0.0,
                                        op0=ALU.mult, op1=ALU.add, accum_out=acc[:, 0:1]).then_inc(ada_used, 1)
                                    dve.drain()
                                    nc.vector.tensor_tensor(mod[:, bass.ds(next_layer(l, MODS, k), 1)], acc[:, 0:1],
                                                            cols[:, bass.ds(next_layer(l, COLS, k + C_BADA), 1)], ALU.add)
                                    dve.drain()
                    dve.drain()
                    if not last:
                        with dve.If(q < 1):
                            nc.vector.memset(M[:, :, :], 0.0)
                        dve.drain()
                        for m in range(KT):
                            n = q * (FQ // 4) + (2 * UPQ // 4 + m // 4)
                            ready(l, n, U_FFN, m % 4)
                            nc.vector.tensor_tensor(M[:, m], M[:, m], ps[4 + m % 4][:, :], ALU.add
                                                    ).then_inc(dn_added, 1)
                        dve.drain()

                def dn_add(k):
                    u, cols_ = wo_item(k)
                    if 4 <= k < 8:
                        dve.wait_ge(half_done, l * 8 + (k + 1))
                    else:
                        ready(l, (QUARTERS - 1) * (FQ // 4) + (2 * UPQ // 4 + u // 4), U_FFN, u % 4)
                    nc.vector.tensor_tensor(M[:, u, cols_], M[:, u, cols_], ps[k % 2][:, cols_], ALU.add
                                            ).then_inc(dn_added, 1)

                with dve.Fori(0, QUARTERS - 1) as q:
                    quarter(q, False)
                quarter(QUARTERS - 1, True)
                nc.vector.memset(T[:, 2], 0.0)
                post_coef(l, 1)
                for k in range(8):
                    dn_add(k)
                    add_squares(2 * l + 1, k)
                y_inverse(2 * l + 1, 0)
                for k in range(8, 11):
                    dn_add(k)
                    post(2 * l + 1, 0, POSTED[k])
                with dve.If(l < DEPTH - 1):
                    modulation(next_layer(l, MODS, SHIFT_M), next_layer(l, MODS, SCALE_M),
                               next_layer(l, COLS, C_GPREM))
                    dn_add(11)
                    x_inverse(2 * l + 2, 0)
                    norm(2 * l + 2, 0, {2: lambda: y_inverse(2 * l + 1, 1)})
                with dve.Else():
                    dn_add(11)
                    y_inverse(2 * l + 1, 1)
                    for m in range(0, KT, 2):
                        post(2 * l + 1, 1, (m, m + 1))

        @block.tensor
        def _(pe):
            def mm3(out, wh, wl, xh, xl, start, stop):
                nc.tensor.matmul(out, wh, xh, start=start, stop=False)
                nc.tensor.matmul(out, wh, xl, start=False, stop=False)
                return nc.tensor.matmul(out, wl, xh, start=False, stop=stop)

            def unit(l, i, base, s, bank, src, tiles=None, part=None, between={}, last_part=True):
                t = slice(0, S) if part is None else half(part)
                pe.wait_ge(w_split, l * UNITS + i * 4 + (base + s + 1))
                for k in range(KT):
                    if k in between:
                        between[k]()
                    if tiles:
                        pe.wait_ge(tiles[0], tiles[1] + (k + 1))
                    last = mm3(ps[bank][:, t], WH[:, s, k], WL[:, s, k], src[0][:, k, t], src[1][:, k, t],
                               k == 0, k == KT - 1)
                if last_part:
                    last.then_inc(half_done if part == 0 else unit_done, 1)

            def together(l, i, base, units, banks, src, tiles, part=None, between={}):
                t = slice(0, S) if part is None else half(part)
                for k in range(KT):
                    if k in between:
                        between[k]()
                    pe.wait_ge(tiles[0], tiles[1] + (k + 1))
                    for s in units:
                        if k == 0:
                            pe.wait_ge(w_split, l * UNITS + i * 4 + (base + s + 1))
                        last = mm3(ps[banks[s]][:, t], WH[:, s, k], WL[:, s, k], src[0][:, k, t], src[1][:, k, t],
                                   k == 0, k == KT - 1)
                        if k == KT - 1 and part != 0:
                            last.then_inc(unit_done, 1)

            H, A, O = (HH, HL), (AH, AL), (OH, OL)

            def row_sum(bank, hf, sq, start, stop):
                for c in range(2):
                    last = nc.tensor.matmul(ps[bank][:, hf * HALF + c:hf * HALF + c + 1],
                                            sq[:, hf * HALF + c * P:hf * HALF + (c + 1) * P], ones[:, 0:1],
                                            start=start and c == 0, stop=stop and c == 1, skip_group_check=True)
                return last

            def x_sum(n, hf, ms):
                for m in ms:
                    pe.wait_ge(xsq, (n * 2 + hf) * KT + (m + 1))
                    last = row_sum(X_BANKS[hf], hf, M[:, m], m == 0, m == KT - 1)
                if m == KT - 1:
                    last.then_inc(xsum, 1)

            def x_total(n):
                pe.wait_ge(xsq_added, n)
                row_sum(X_BANKS[1], 1, M[:, 0], True, True).then_inc(xsum, 1)

            def y_first(n):
                pe.wait_ge(y_acc, n * 8 + (8 + 2))
                row_sum(Y_BANKS[1], 1, T[:, 2], True, False)
                row_sum(Y_BANKS[0], 0, T[:, 2], True, True).then_inc(y_sum, 1)

            def y_add(n, k):
                pe.wait_ge(y_sq, n * 12 + (k + 1))
                row_sum(Y_BANKS[1], 1, T[:, k % 2], False, k == 11).then_inc(y_tail, 1)

            def broadcast(bank, hf, inverted, done, count):
                pe.wait_ge(inverted, count)
                for c in range(2):
                    last = nc.tensor.matmul(ps[bank][:, hf * HALF + c * P:hf * HALF + (c + 1) * P], ones[:, :],
                                            diag[:, c], start=True, stop=True)
                last.then_inc(done, 1)

            def x_broadcast(n, hf):
                broadcast(X_BANKS[hf], hf, x_inv, x_bc, n * 2 + (hf + 1))

            def y_broadcast(n, hf):
                broadcast(Y_BANKS[hf], hf, y_inv, y_bc, n * 2 + (hf + 1))

            def last_outputs(n, first, output, next_sum):
                for k in range(first, 12):
                    between = {}
                    if k == 8:
                        between[5] = lambda: y_first(n)
                    if k > 8:
                        between[5] = lambda k=k: y_add(n, k - 1)
                    if k == 11:
                        between[2] = lambda: next_sum(POSTED[8])
                        between[7] = lambda: next_sum(POSTED[9])
                    output(k, between)
                    if k == 8:
                        y_broadcast(n, 0)
                next_sum(POSTED[10])
                y_add(n, 11)

            def begin(l, base, n, before, total, spread):
                together(l, 0, base, range(3), range(4), H, (h_ready, n * 2 * KT), 0, {2: before})
                unit(l, 0, base, 3, 3, H, None, 0, {5: total, 7: spread}, last_part=False)
                together(l, 0, base, (0, 1), range(4), H, (h_ready, (n * 2 + 1) * KT), 1)

            pe.sem_inc(unit_done, RING)
            pe.sem_inc(v_tr, 4)
            pe.sem_inc(vb_tr, 1)
            pe.wait_ge(dve_consts, 1)
            for hf in range(2):
                x_sum(0, hf, range(KT))
            for hf in range(2):
                x_broadcast(0, hf)
            pe.sem_inc(pe_stage, 1)
            with pe.Fori(0, DEPTH) as l:

                def v_transpose(i, s):
                    pe.wait_ge(v_gelu, l * KT + i * 4 + (s + 1))
                    pe.wait_ge(v_copied, l * KT + i * 4 + (s + 1))
                    for c in range(NC):
                        last = nc.tensor.transpose(ps[4 + s % 2][:, c * P:(c + 1) * P], T[:, s, c * P:(c + 1) * P],
                                                   ident[:, :])
                    last.then_inc(v_tr, 1)

                pe.wait_ge(dn_added, l * DN_ITEMS + 2)

                def before():
                    with pe.If(l > 0):
                        y_broadcast(2 * l - 1, 1)

                def total():
                    with pe.If(l > 0):
                        x_total(2 * l)

                def spread():
                    with pe.If(l > 0):
                        x_broadcast(2 * l, 1)

                begin(l, U_V, 2 * l, before, total, spread)
                unit(l, 0, U_V, 2, 2, H, None, 1)
                v_transpose(0, 0)
                unit(l, 0, U_V, 3, 3, H, None, 1)
                v_transpose(0, 1)
                v_transpose(0, 2)
                for s in range(4):
                    unit(l, 1, U_V, s, s, H)
                    v_transpose(1 if s else 0, (s - 1) % 4)
                v_transpose(1, 3)
                def spatial(g):
                    if g >= 2:
                        pe.wait_ge(a_ready, l * KT + g - 1 + 4)
                    for c in range(NC):
                        last = mm3(ps[4 + g % 2][:, c * P:(c + 1) * P], AH[:, g, c * P:(c + 1) * P],
                                   AL[:, g, c * P:(c + 1) * P], WSH[:, g * P:(g + 1) * P],
                                   WSL[:, g * P:(g + 1) * P], True, True)
                    last.then_inc(f_done, 1)

                for u in range(KT):
                    if u >= 4:
                        pe.wait_ge(u_gelu, l * KT + u - 3)
                    unit(l, u // 4, U_U, u % 4, u % 4, H)
                    if u == 3:
                        pe.wait_ge(ws_split, l + 1)
                        pe.wait_ge(vn_ready, l * NC + NC)
                        spatial(0)
                        spatial(1)
                    if u > 3:
                        spatial(u - 2)

                def suffix(h, js):
                    for j in js:
                        pe.wait_ge(sp_ready, l * 32 + h * 4 + (NC - j))
                        for k in range(j, NC):
                            at = (k - j) * P
                            for part in (SPH[k], SPL[k]):
                                last = nc.tensor.matmul(ps[4 + j][:, at:n_keys(j)],
                                                        ntri[:, :] if k == j else nones[:, :], part, start=False,
                                                        stop=True, skip_group_check=True)
                        last.then_inc(sfx, 1)

                def values(h):
                    pe.wait_ge(o_split, l * HEADS + h + 1)
                    pe.wait_ge(vb_split, l * HEADS + h + 1 + 1)
                    for j in (3, 2, 1, 0):
                        pe.wait_ge(attn_ready, l * 32 + h * 4 + (NC - j))
                        out = ps[3][:, j * P:S]
                        vh, vl = VH[:, j * P:(j + 1) * P], VL[:, j * P:(j + 1) * P]
                        nc.tensor.matmul(out, vh, ATH[j], start=j == NC - 1, stop=False, skip_group_check=True)
                        nc.tensor.matmul(out, vh, ATL[j], start=False, stop=False, skip_group_check=True)
                        last = nc.tensor.matmul(out, vl, ATH[j], start=False, stop=j == 0, skip_group_check=True)
                    last.then_inc(av_done, 1)

                def scores(h):
                    pe.wait_ge(q_split, l * HEADS + h + 1 + 1)
                    pe.wait_ge(k_split, l * HEADS + h + 1 + 1)
                    for j in (3, 2, 1, 0):
                        mm3(ps[4 + j][:, 0:n_keys(j)], KH[:, j * P:(j + 1) * P], KL[:, j * P:(j + 1) * P],
                            QH[:, j * P:S], QL[:, j * P:S], True, True).then_inc(z_done, 1)

                def head(h, first):
                    unit(l, h, U_HEAD, 0, 0, H)
                    if first:
                        spatial(6)
                    if not first:
                        suffix(h - 1, (3, 2))
                        pe.wait_ge(ao_evac, l * HEADS + h)
                    unit(l, h, U_HEAD, 1, 1, H)
                    if first:
                        spatial(7)
                    if not first:
                        suffix(h - 1, (1, 0))
                    pe.wait_ge(q_evac, l * HEADS + h + 1)
                    unit(l, h, U_HEAD, 2, 0, H)
                    if first:
                        pe.wait_ge(a_ready, l * KT + KT + 4)
                    else:
                        values(h - 1)
                    scores(h)
                    pe.wait_ge(k_evac, l * HEADS + h + 1)
                    unit(l, h, U_HEAD, 3, 1, A)
                    pe.wait_ge(vb_evac, l * HEADS + h + 1)
                    pe.wait_ge(vb_split, l * HEADS + h + 1)
                    for c in range(NC):
                        last = nc.tensor.transpose(ps[2][:, c * P:(c + 1) * P], T[:, 2, c * P:(c + 1) * P],
                                                   ident[:, :])
                    last.then_inc(vb_tr, 1)

                pe.wait_ge(u_gelu, l * KT + KT - 1)
                head(0, True)
                with pe.Fori(1, HEADS) as h:
                    head(h, False)
                pe.wait_ge(ao_evac, l * HEADS + HEADS)
                for u in range(KT):
                    if u == 2:
                        pe.wait_ge(vb_split, l * HEADS + HEADS + 1)
                    if u >= 4:
                        pe.wait_ge(ga_sig, l * KT + u - 3)
                    unit(l, u // 4, U_GA, u % 4, GA_BANKS[u % 4], H)
                    if u == 0:
                        suffix(HEADS - 1, (3, 2))
                    if u == 1:
                        suffix(HEADS - 1, (1, 0))
                    if u == 2:
                        values(HEADS - 1)
                pe.wait_ge(o_split, l * HEADS + HEADS + 1)
                pe.sem_inc(pe_stage, 1)
                with pe.Fori(0, KT // 2) as i:
                    for s in range(4):
                        pe.wait_ge(merged, l * KT + i * 2 + (s // 2 + 1))
                        unit(l, i, U_GB, s, GB_BANKS[s], O if s % 2 else H)
                def wo_out(k, between):
                    u, _ = wo_item(k)
                    pe.wait_ge(wo_evac, l * 12 + (k + 1))
                    unit(l, u // 4, U_O, u % 4, k % 2, A, None if k else (merged, l * KT + 2),
                         None if k < 4 else k // 8, between)

                last_outputs(2 * l, 0, wo_out, lambda ms: x_sum(2 * l + 1, 0, ms))
                x_broadcast(2 * l + 1, 0)

                def up(q, i, units=range(4), part=None):
                    for s in units:
                        pe.wait_ge(conved, ((l * QUARTERS + q) * UPQ + i * 2) * 2 + (s + 1))
                        unit(l, q * (FQ // 4) + i, U_FFN, s, s, H, None, part)

                def down_two(q, added, banks):
                    pe.wait_ge(dn_added, l * DN_ITEMS + added + 2)
                    together(l, q * (FQ // 4) + 2 * UPQ // 4, U_FFN, (0, 1), banks, O,
                             (g_ready, (l * QUARTERS + q) * UPQ + 2))

                def down(q, k, added, bank, part=None, between={}):
                    u = k if part is None else 4 + k % 4
                    pe.wait_ge(dn_added, l * DN_ITEMS + added + (k + 1 if bank < 4 else k - 1))
                    unit(l, q * (FQ // 4) + (2 * UPQ // 4 + u // 4), U_FFN, u % 4, bank, O, None, part, between)

                pe.wait_ge(wo_evac, l * 12 + (12 + 2))
                pe.wait_ge(conved, l * PAIRS * 2 + 4)
                begin(l, U_FFN, 2 * l + 1, lambda: y_broadcast(2 * l, 1), lambda: x_total(2 * l + 1),
                      lambda: x_broadcast(2 * l + 1, 1))
                up(0, 0, (2, 3), 1)
                pe.sem_inc(pe_stage, 1)
                with pe.Fori(1, UPQ // 2) as i:
                    up(0, i)
                down_two(0, 0, (4, 5))
                for k in range(2, KT):
                    down(0, k, 0, 4 + k % 4)
                with pe.Fori(1, QUARTERS - 1) as q:
                    with pe.Fori(0, UPQ // 2) as i:
                        up(q, i)
                    down_two(q, q * KT, (4, 5))
                    for k in range(2, KT):
                        down(q, k, q * KT, 4 + k % 4)
                with pe.Fori(0, UPQ // 2) as i:
                    up(QUARTERS - 1, i)
                pe.wait_ge(conved, (l + 1) * PAIRS * 2 + (4 - 2))
                down_two(QUARTERS - 1, (QUARTERS - 1) * KT, (0, 1))
                def next_sum(ms):
                    with pe.If(l < DEPTH - 1):
                        x_sum(2 * l + 2, 0, ms)

                last_outputs(2 * l + 1, 2, lambda k, between: down(QUARTERS - 1, k, (QUARTERS - 1) * KT, k % 2,
                                                                   None if k < 4 else k // 8, between), next_sum)
                with pe.If(l < DEPTH - 1):
                    x_broadcast(2 * l + 2, 0)
                with pe.Else():
                    y_broadcast(2 * l + 1, 1)


def kernel(**inputs):
    import numpy as np
    import concourse.bacc as bacc
    from concourse.bass_utils import run_bass_kernel_spmd as run

    a = {k: np.asarray(v) for k, v in inputs.items()}
    L = DEPTH

    def units(w):
        l_, k, n = w.shape
        return w.reshape(l_, k // P, P, n // P, P).transpose(0, 3, 2, 1, 4)

    w_in = units(a["w_in"]).reshape(L, -1, P, KT * P)
    u_a, v_a, q, k, v, g_a, g_b = (w_in[:, 8 * i:8 * i + 8] for i in range(7))
    flat = lambda w: units(w).reshape(L, -1, P, KT * P)
    a_out, b_out, w_o, up = flat(a["w_a_out"]), flat(a["w_b_out"]), flat(a["w_o"]), flat(a["w_up"])
    pair = lambda *w: np.stack(w, axis=2).reshape(L, -1, P, KT * P)
    up = pair(up[:, :PAIRS], up[:, PAIRS:])
    parts = [v_a, u_a, pair(q, k, v, a_out), g_a, pair(g_b, b_out), w_o]
    for i in range(QUARTERS):
        parts.append(up[:, 2 * UPQ * i:2 * UPQ * (i + 1)])
        parts.append(flat(a["w_down"][:, i * UPQ * P:(i + 1) * UPQ * P]))
    stream = np.ascontiguousarray(np.concatenate(parts, axis=1)).reshape(L * UNITS, P, KT * P)

    vec = lambda x: x.reshape(L, -1, P)
    cols_h = np.concatenate([vec(a[n]) for n in ("b_ada", "g_pre_mix", "g_post_mix", "g_pre_ffn", "g_post_ffn",
                                                 "g_sgu", "conv_b", "conv_w")], axis=1)
    arrays = {
        "xT": a["x"][0].T.reshape(KT, P, S).transpose(1, 0, 2),
        "cvec": a["c"].reshape(1, D),
        "w_stream": stream,
        "w_ada_rows": a["w_ada"].transpose(0, 2, 1).reshape(L * MODS, P, D),
        "cols_d": cols_h.reshape(L * COLS, P).T,
        "w_sp": a["w_spatial"].transpose(0, 3, 1, 2).reshape(L, P, KT * P),
        "b_sp": a["b_spatial"].reshape(L, KT * P),
    }
    arrays = {k_: np.ascontiguousarray(v_) for k_, v_ in arrays.items()}
    nc = bacc.Bacc("TRN2", target_bir_lowering=False, num_devices=1, dynamic_dma_scratch_size=1024)
    args = [nc.dram_tensor(n, x.shape, mybir.dt.from_np(x.dtype), kind="ExternalInput").ap()
            for n, x in arrays.items()]
    out = nc.dram_tensor("outT", (P, KT, S), F32, kind="ExternalOutput").ap()
    build(nc, *args, out)
    r = run(nc, [arrays], core_ids=[0])
    y = r.results[0]["outT"]
    return y.transpose(1, 0, 2).reshape(D, S).T.reshape(1, S, D)
```
